# Optimizing a Trainium2 kernel written in Bass

```python
import jax, jax.numpy as jnp
from jax import lax
import numpy as np

D_MODEL = 2048
BATCH = 1
SEQ = 512
DEPTH = 1
DEC_BATCH = 8
DEC_SEQ = 16
PAST_LEN = 128

CHUNK = 64
HEAD_DIM = 64
A_HEADS = 16
A_PREV_CHUNKS = 8
A_REL_CLIP = 128
B_Q_HEADS = 16
B_KV_HEADS = 2
B_WINDOW = 128
B_PREV_CHUNKS = B_WINDOW // CHUNK
A_WIDTH = A_HEADS * HEAD_DIM
B_WIDTH = B_Q_HEADS * HEAD_DIM
B_KV_WIDTH = B_KV_HEADS * HEAD_DIM
IN_SPLITS = (A_WIDTH, A_WIDTH, A_WIDTH, B_WIDTH, B_KV_WIDTH, B_KV_WIDTH, D_MODEL, D_MODEL)
IN_COLS = sum(IN_SPLITS)
PEER_HEADS = 8
PEER_KEYS = 128
PEER_EXPERTS = PEER_KEYS * PEER_KEYS
PEER_QDIM = 256
PEER_TOPK = 16
PEER_BLOCK = 128
LN_EPS = 1e-5
DEEPNORM_ALPHA = (2 * DEPTH) ** 0.25
DEEPNORM_BETA = (8 * DEPTH) ** -0.25

kernel_name = "hybrid_chunk_band_attn_peer_streaming_step"

def layer_norm(x, g, b):
    xf = x.astype(jnp.float32)
    mu = jnp.mean(xf, axis=-1, keepdims=True)
    var = jnp.mean(jnp.square(xf - mu), axis=-1, keepdims=True)
    return ((xf - mu) * lax.rsqrt(var + LN_EPS) * g.astype(jnp.float32) + b.astype(jnp.float32)).astype(x.dtype)

def split_projection(x, w_in):
    p = jnp.einsum('bsd,de->bse', x, w_in)
    offs = np.cumsum(IN_SPLITS)[:-1].tolist()
    qa, ka, va, qb, kb, vb, ga, gb = jnp.split(p, offs, axis=-1)
    hd = lambda t: t.reshape(t.shape[:2] + (-1, HEAD_DIM))
    return hd(qa), hd(ka), hd(va), hd(qb), hd(kb), hd(vb), ga, gb

def rel_bias(rel_table, dist):
    idx = jnp.clip(dist, -A_REL_CLIP, A_REL_CLIP) + A_REL_CLIP
    return jnp.take(rel_table, idx, axis=1).astype(jnp.float32)

def alibi_bias(dist):
    slopes = jnp.exp2(-8.0 * jnp.arange(1, B_Q_HEADS + 1, dtype=jnp.float32) / B_Q_HEADS)
    return -slopes[:, None, None] * jnp.abs(dist).astype(jnp.float32)[None]

def band_attention_core(q, kb, vb, bias, valid, sink):
    b, n, tq, h, dh = q.shape
    hk = kb.shape[3]
    g = h // hk
    qg = q.reshape(b, n, tq, hk, g, dh)
    s = jnp.einsum('bnqkgd,bnskd->bkgnqs', qg, kb).astype(jnp.float32) * (dh ** -0.5)
    s = s + bias.reshape(hk, g, 1, tq, -1)
    s = jnp.where(valid[:, None, :], s, -jnp.inf)
    m = jnp.max(s, axis=-1, keepdims=True)
    if sink is not None:
        sk = sink.astype(jnp.float32).reshape(hk, g, 1, 1, 1)
        m = jnp.maximum(m, sk)
        p = jnp.exp(s - m)
        den = jnp.sum(p, axis=-1, keepdims=True) + jnp.exp(sk - m)
    else:
        p = jnp.exp(s - m)
        den = jnp.sum(p, axis=-1, keepdims=True)
    p = (p / den).astype(vb.dtype)
    o = jnp.einsum('bkgnqs,bnskd->bnqkgd', p, vb)
    return o.reshape(b, n, tq, h * dh)

def band_attention_prompt(q, k, v, n_prev, bias_fn, sink):
    b, s, h, dh = q.shape
    hk = k.shape[2]
    nc = s // CHUNK
    pad = n_prev * CHUNK
    tk = (n_prev + 1) * CHUNK
    kp = jnp.pad(k, ((0, 0), (pad, 0), (0, 0), (0, 0))).reshape(b, nc + n_prev, CHUNK, hk, dh)
    vp = jnp.pad(v, ((0, 0), (pad, 0), (0, 0), (0, 0))).reshape(b, nc + n_prev, CHUNK, hk, dh)
    idx = jnp.arange(nc)[:, None] + jnp.arange(n_prev + 1)[None, :]
    kb = kp[:, idx].reshape(b, nc, tk, hk, dh)
    vb = vp[:, idx].reshape(b, nc, tk, hk, dh)
    key_pos = (jnp.arange(nc)[:, None] - n_prev) * CHUNK + jnp.arange(tk)[None, :]
    valid = key_pos >= 0
    dist = jnp.arange(CHUNK)[:, None] + pad - jnp.arange(tk)[None, :]
    o = band_attention_core(q.reshape(b, nc, CHUNK, h, dh), kb, vb, bias_fn(dist), valid, sink)
    return o.reshape(b, s, h * dh)

def band_attention_sample(q, k_new, v_new, k_cache, v_cache, bias_fn, sink):
    b, t, h, dh = q.shape
    L = k_cache.shape[1]
    kb = jnp.concatenate([k_cache.astype(k_new.dtype), k_new], axis=1)[:, None]
    vb = jnp.concatenate([v_cache.astype(v_new.dtype), v_new], axis=1)[:, None]
    dist = jnp.arange(t)[:, None] + L - jnp.arange(L + t)[None, :]
    valid = jnp.ones((1, L + t), dtype=bool)
    o = band_attention_core(q[:, None], kb, vb, bias_fn(dist), valid, sink)
    return o.reshape(b, t, h * dh)

def mixer_merge(ya, yb, ga, gb, w_proj_a, w_proj_b, w_out):
    za = jnp.einsum('bse,ed->bsd', ya, w_proj_a)
    zb = jnp.einsum('bse,ed->bsd', yb, w_proj_b)
    m = jax.nn.sigmoid(ga) * za + jax.nn.sigmoid(gb) * zb
    return jnp.einsum('bsd,de->bse', m, w_out)

def peer_tokens(xt, w_query, sub_keys_1, sub_keys_2, u_table, v_table):
    n = xt.shape[0]
    q = (xt @ w_query).reshape(n, PEER_HEADS, 2, PEER_QDIM // 2)
    s1 = jnp.einsum('nhd,kd->nhk', q[:, :, 0], sub_keys_1).astype(jnp.float32)
    s2 = jnp.einsum('nhd,kd->nhk', q[:, :, 1], sub_keys_2).astype(jnp.float32)
    v1, i1 = lax.top_k(s1, PEER_TOPK)
    v2, i2 = lax.top_k(s2, PEER_TOPK)
    cand = (v1[..., :, None] + v2[..., None, :]).reshape(n, PEER_HEADS, PEER_TOPK * PEER_TOPK)
    sc, ci = lax.top_k(cand, PEER_TOPK)
    e1 = jnp.take_along_axis(i1, ci // PEER_TOPK, axis=-1)
    e2 = jnp.take_along_axis(i2, ci % PEER_TOPK, axis=-1)
    experts = e1 * PEER_KEYS + e2
    gate = jax.nn.softmax(sc, axis=-1)
    u = jnp.take(u_table, experts, axis=0)
    act = jax.nn.gelu(jnp.einsum('nhkd,nd->nhk', u, xt).astype(jnp.float32), approximate=False)
    w = (gate * act).astype(xt.dtype)
    v = jnp.take(v_table, experts, axis=0)
    return jnp.einsum('nhk,nhkd->nd', w, v)

def peer_layer(x, w_query, sub_keys_1, sub_keys_2, u_table, v_table):
    xb = x.reshape(-1, PEER_BLOCK, x.shape[-1])
    out = lax.map(lambda blk: peer_tokens(blk, w_query, sub_keys_1, sub_keys_2, u_table, v_table), xb)
    return out.reshape(x.shape)

def setup_inputs(seed: int = 0) -> dict:
    key = jax.random.key(seed)
    ks = jax.random.split(key, 24)
    f32 = jnp.float32
    nrm = lambda k, shape: jax.random.normal(k, shape, dtype=f32)
    la = min(A_PREV_CHUNKS * CHUNK, PAST_LEN)
    lb = min(B_WINDOW, PAST_LEN)
    col_scale = np.ones((IN_COLS,), dtype=np.float32)
    offs = np.cumsum((0,) + IN_SPLITS)
    col_scale[offs[2]:offs[3]] = DEEPNORM_BETA
    col_scale[offs[5]:offs[6]] = DEEPNORM_BETA
    w_in = nrm(ks[4], (D_MODEL, IN_COLS)) * (D_MODEL ** -0.5) * jnp.asarray(col_scale)
    return {
        "x_prompt": nrm(ks[0], (BATCH, SEQ, D_MODEL)),
        "x_sample": nrm(ks[1], (DEC_BATCH, DEC_SEQ, D_MODEL)),
        "cache_a_k": nrm(ks[2], (DEC_BATCH, la, A_HEADS, HEAD_DIM)),
        "cache_a_v": nrm(ks[3], (DEC_BATCH, la, A_HEADS, HEAD_DIM)) * DEEPNORM_BETA,
        "cache_b_k": nrm(ks[5], (DEC_BATCH, lb, B_KV_HEADS, HEAD_DIM)),
        "cache_b_v": nrm(ks[6], (DEC_BATCH, lb, B_KV_HEADS, HEAD_DIM)) * DEEPNORM_BETA,
        "w_in": w_in,
        "rel_bias_table": 0.5 * nrm(ks[7], (A_HEADS, 2 * A_REL_CLIP + 1)),
        "b_sinks": nrm(ks[8], (B_Q_HEADS,)),
        "w_proj_a": nrm(ks[9], (A_WIDTH, D_MODEL)) * (A_WIDTH ** -0.5) * DEEPNORM_BETA,
        "w_proj_b": nrm(ks[10], (B_WIDTH, D_MODEL)) * (B_WIDTH ** -0.5) * DEEPNORM_BETA,
        "w_out": nrm(ks[11], (D_MODEL, D_MODEL)) * (D_MODEL ** -0.5) * DEEPNORM_BETA,
        "ln1_g": 1.0 + 0.05 * nrm(ks[12], (D_MODEL,)),
        "ln1_b": 0.02 * nrm(ks[13], (D_MODEL,)),
        "peer_w_query": nrm(ks[14], (D_MODEL, PEER_HEADS * PEER_QDIM)) * (D_MODEL ** -0.5),
        "peer_sub_keys_1": nrm(ks[15], (PEER_KEYS, PEER_QDIM // 2)) * ((PEER_QDIM // 2) ** -0.5),
        "peer_sub_keys_2": nrm(ks[16], (PEER_KEYS, PEER_QDIM // 2)) * ((PEER_QDIM // 2) ** -0.5),
        "peer_u": nrm(ks[17], (PEER_EXPERTS, D_MODEL)) * (D_MODEL ** -0.5),
        "peer_v": nrm(ks[18], (PEER_EXPERTS, D_MODEL)) * DEEPNORM_BETA,
        "ln2_g": 1.0 + 0.05 * nrm(ks[19], (D_MODEL,)),
        "ln2_b": 0.02 * nrm(ks[20], (D_MODEL,)),
    }

def reference(x_prompt, x_sample, cache_a_k, cache_a_v, cache_b_k, cache_b_v, w_in, rel_bias_table, b_sinks,
              w_proj_a, w_proj_b, w_out, ln1_g, ln1_b, peer_w_query, peer_sub_keys_1, peer_sub_keys_2,
              peer_u, peer_v, ln2_g, ln2_b):
    bias_a = lambda d: rel_bias(rel_bias_table, d)
    peer_args = (peer_w_query, peer_sub_keys_1, peer_sub_keys_2, peer_u, peer_v)

    qa, ka, va, qb, kb, vb, ga, gb = split_projection(x_prompt, w_in)
    ya = band_attention_prompt(qa, ka, va, A_PREV_CHUNKS, bias_a, None)
    yb = band_attention_prompt(qb, kb, vb, B_PREV_CHUNKS, alibi_bias, b_sinks)
    h_p = layer_norm(DEEPNORM_ALPHA * x_prompt + mixer_merge(ya, yb, ga, gb, w_proj_a, w_proj_b, w_out), ln1_g, ln1_b)
    y_prompt = layer_norm(DEEPNORM_ALPHA * h_p + peer_layer(h_p, *peer_args), ln2_g, ln2_b)
    la_p = min(A_PREV_CHUNKS * CHUNK, x_prompt.shape[1])
    lb_p = min(B_WINDOW, x_prompt.shape[1])

    qa_s, ka_s, va_s, qb_s, kb_s, vb_s, ga_s, gb_s = split_projection(x_sample, w_in)
    ya_s = band_attention_sample(qa_s, ka_s, va_s, cache_a_k, cache_a_v, bias_a, None)
    yb_s = band_attention_sample(qb_s, kb_s, vb_s, cache_b_k, cache_b_v, alibi_bias, b_sinks)
    h_s = layer_norm(DEEPNORM_ALPHA * x_sample + mixer_merge(ya_s, yb_s, ga_s, gb_s, w_proj_a, w_proj_b, w_out), ln1_g, ln1_b)
    n_s = h_s.shape[0] * h_s.shape[1]
    ffn_s = peer_tokens(h_s.reshape(n_s, D_MODEL), *peer_args).reshape(h_s.shape)
    y_sample = layer_norm(DEEPNORM_ALPHA * h_s + ffn_s, ln2_g, ln2_b)

    return (y_prompt, y_sample, ka[:, -la_p:], va[:, -la_p:], kb[:, -lb_p:], vb[:, -lb_p:], ka_s, va_s, kb_s, vb_s)


_drawn_inputs = setup_inputs


def setup_inputs(seed=0):
    import zlib

    import numpy as np

    out = dict(_drawn_inputs(seed))
    spreads = {}
    factors = {'rel_bias_table': 2.809, 'b_sinks': 4.613, 'ln2_b': 2.874}
    for name, (base, spread) in spreads.items():
        noise = np.random.default_rng([zlib.crc32(name.encode()), seed]).standard_normal(out[name].shape)
        drawn = base * np.exp(spread * noise) if base else spread * noise
        out[name] = __import__('jax').numpy.asarray(drawn.astype(out[name].dtype))
    for name, factor in factors.items():
        out[name] = (out[name] * factor).astype(out[name].dtype)
    return out
```

```python
from contextlib import ExitStack

import numpy as np
import concourse.bass as bass
from concourse import mybir

P = 128
D = 2048
KT_N = D // P
SEQ, DEC_B, DEC_T = 512, 8, 16
T = SEQ + DEC_B * DEC_T
HALF = T // 2
NB = T // P
PAST = 128
HD = 64
PAIRS = 8
PH, TOPK, KEYS = 8, 16, 128
EPS = 1e-5
ALPHA = float(2.0 ** 0.25)
SCALE = HD ** -0.5
NEG = -1e30
EG = 4
GROUPS = KEYS // EG
GT = 40
GBLK = T // GT

N_QKV, N_GATE, N_PROJ, N_OUT, N_QUERY = 34, 32, 16, 16, 16
U_QKV = 0
U_GATE = U_QKV + N_QKV
U_PROJ = U_GATE + N_GATE
U_OUT = U_PROJ + N_PROJ
U_QUERY = U_OUT + N_OUT
U_PEER = U_QUERY + N_QUERY
UNITS = U_PEER + 2 * EG * GROUPS
ROW_KB, ROW_QA, ROW_QB = 16, 18, 26


class Own:

    def __init__(self, eng, sem, apart):
        self.eng, self.sem, self.apart, self.n, self.off = eng, sem, apart, 0, 0

    def done(self, ins):
        ins.then_inc(self.sem, 1)
        self.n += 1

    def wait(self):
        self.eng.wait_ge(self.sem, self.off + self.n)

    def wait_apart(self):
        self.wait()
        self.eng.sem_inc(self.apart, 1)

    def enter(self, i, per):
        self.start, self.per = self.n, per
        self.off = i * per

    def leave(self, trips):
        assert self.n - self.start == self.per, (self.n - self.start, self.per)
        self.n, self.off = self.start + self.per * trips, 0


def build(nc, x_t, wstream, cka, cva, ckb, cvb, rext, negs, bp_b, bs_b, sinks, lnp, subk, consts, pt_out, y_out):
    f32, f32r, u32 = mybir.dt.float32, mybir.dt.float32r, mybir.dt.uint32
    ALU, ACT = mybir.AluOpType, mybir.ActivationFunctionType
    AX = mybir.AxisListType
    ds = bass.ds

    with ExitStack() as ctx:
        def dram(name, shape):
            return nc.dram_tensor(name, shape, f32).ap()

        def sb(name, shape, dt=f32):
            return ctx.enter_context(nc.sbuf_tensor(name, shape, dt))

        def sem(name):
            return ctx.enter_context(nc.semaphore(name))

        g_s = dram("gate_scratch", (N_GATE, P, T))
        y_s = dram("attn_scratch", (KT_N, P, T))
        m_s = dram("merge_scratch", (KT_N, P, T))
        bp_a = dram("bias_prompt_a", (16, P, 512))
        bs_a = dram("bias_sample_a", (16, P, 144))
        G_s = dram("gate_matrix", (GBLK, P, KEYS, GT))

        raw = [sb(f"w_raw{s}", [P, D]) for s in range(2)]
        w_hi = [sb(f"w_hi{s}", [P, D], f32r) for s in range(2)]
        w_lo = [sb(f"w_lo{s}", [P, D], f32r) for s in range(2)]
        mv_hi = sb("mv_hi", [P, KT_N, T], f32r)
        mv_lo = sb("mv_lo", [P, KT_N, T], f32r)
        R = sb("work", [P, KT_N * T])
        ww_hi = sb("ww_hi", [P, EG, T], f32r)
        ww_lo = sb("ww_lo", [P, EG, T], f32r)
        W2 = sb("work2", [P, 6 * T])
        cst = sb("cst", [P, 4 * P])
        subkt = sb("subkt", [P, 2 * KEYS])
        sinkt = sb("sinkt", [P, 16])
        lnt = sb("lnt", [P, 4 * KT_N])
        small = sb("small", [P, 16])

        ident, ones, iota, bmask = (cst[:, P * i:P * i + P] for i in range(4))
        Rt = R[:, :].rearrange("p (k t) -> p k t", k=KT_N)

        def area(at, n):
            return R[:, at:at + n]
        ck_t, cv_t = area(0, 1024), area(1024, 1024)
        bp_t = area(2048, 1024).rearrange("p (h c) -> p h c", h=2)
        bs_t = area(3072, 288).rearrange("p (h c) -> p h c", h=2)
        q_t, k_t, v_t = area(3360, T), area(4000, T), area(4640, T)
        vn = area(5280, T)
        s_sb = [area(5920, 512), area(6432, 512)]
        pt_sb = [area(6944, 512), area(7456, 512)]
        st_sb = [area(7968, P), area(8096, P)]
        y_t = area(8224, T)
        mx = [small[:, s:s + 1] for s in range(2)]
        nmax = [small[:, 2 + s:3 + s] for s in range(2)]
        rsum = [small[:, 4 + s:5 + s] for s in range(2)]
        esink = [small[:, 6 + s:7 + s] for s in range(2)]
        rden = [small[:, 8 + s:9 + s] for s in range(2)]
        den = [small[:, 10 + s:11 + s] for s in range(2)]

        ev = [W2[:, T * s:T * s + T] for s in range(2)]
        gate_t = [W2[:, 2 * T * (s + 1):2 * T * (s + 2)] for s in range(2)]
        x_res = [W2[:, 2 * T + T * s:3 * T + T * s] for s in range(2)]
        mean_t, rstd_t = W2[:, 0:T], W2[:, T:2 * T]
        sq_t = x_res
        pick_t = [W2[:, T * q:T * q + T] for q in range(3)]
        oh1 = W2[:, 3 * T:3 * T + 8 * P].rearrange("p (n e) -> p n e", n=8)
        oh2 = ww_hi[:, :, :].rearrange("p e t -> p (e t)")[:, 0:8 * P].rearrange("p (n e) -> p n e", n=8)
        act_t = ev
        G4 = W2[:, 2 * T:6 * T].rearrange("p (b e t) -> p b e t", b=GBLK, e=EG)

        qe = [area(0, T), area(T, T)]
        sc_sb = [area(1280, T), area(1920, T)]
        sc2 = area(2560, T)
        cand, cand2 = area(3200, 1280), area(4480, 1280)
        val = area(5760, 160).rearrange("p (b s k) -> p b s k", b=NB, s=2)
        idx_f = area(5920, 160).rearrange("p (b s k) -> p b s k", b=NB, s=2)
        pick_g = area(6080, T).rearrange("p (b k) -> p b k", b=NB)
        c_f = [area(6720, 80), area(6800, 80)]
        eq = area(6880, 1280)
        pick_e = [area(8160, T).rearrange("p (b k) -> p b k", b=NB), area(8800, T).rearrange("p (b k) -> p b k", b=NB)]
        idx_u = area(9440, 160).bitcast(u32).rearrange("p (b s k) -> p b s k", b=NB, s=2)
        ci_u = area(9600, 80).bitcast(u32)
        cp_u = [area(9680, 80).bitcast(u32), area(9760, 80).bitcast(u32)]
        psum_g = area(9840, 40)
        top_v = area(9880, 80)
        g_buf = [area(w * GT * KEYS, GT * KEYS).rearrange("p (e t) -> p e t", t=GT) for w in range(2)]

        banks = ctx.enter_context(nc.psum_tensor("banks", [P, 8, 512], f32))

        def acc(s):
            return banks[:, 2 * s:2 * s + 2, 0:HALF]

        def two(ap):
            return ap.rearrange("p (a t) -> p a t", a=2)

        s_bank = [banks[:, 4, :], banks[:, 5, :]]
        t_bank, o_bank = banks[:, 6, :], banks[:, 7, :]

        def sc_parts(s):
            return banks[:, 4 + 2 * s, :], banks[:, 5 + 2 * s, 0:P]

        raw_full = [sem(f"raw_full{s}") for s in range(2)]
        hi_done, split_done, unit_done = sem("hi_done"), sem("split_done"), sem("unit_done")
        mv_in = [sem(f"mv_in{q}") for q in range(4)]
        mvh_done, mv_ready = sem("mvh_done"), sem("mv_ready")
        const_in, tab_done = sem("const_in"), sem("tab_done")
        qkv_evac, gate_evac = sem("qkv_evac"), sem("gate_evac")
        qkv_stored = [sem(f"qkv_stored{s}") for s in range(2)]
        gate_stored = [sem(f"gate_stored{s}") for s in range(2)]
        att_in, s_full, s_taken, nmax_ready, e_ready, p_ready = (
            sem(n) for n in ("att_in", "s_full", "s_taken", "nmax_ready", "e_ready", "p_ready"))
        t_full, t_taken, o_full, o_taken, y_stored = (
            sem(n) for n in ("t_full", "t_taken", "o_full", "o_taken", "y_stored"))
        gate_in = [sem(f"gate_in{s}") for s in range(2)]
        sig_done, za_done, z_taken, msum_done = (sem(n) for n in ("sig_done", "za_done", "z_taken", "msum_done"))
        m_stored = [sem(f"m_stored{s}") for s in range(2)]
        x_in = [sem(f"x_in{s}") for s in range(2)]
        r_done = sem("r_done")
        ln = [{n: sem(f"ln{p}_{n}") for n in ("sum", "centered", "squared", "sq_used", "var", "std", "scaled", "out")}
              for p in range(2)]
        y_out_done = sem("y_out_done")
        res_done = sem("res_done")
        q_evac, sc_full, sc_taken, topk_done = (sem(n) for n in ("q_evac", "sc_full", "sc_taken", "topk_done"))
        gexp_in, gexp_done, picks_done, picks_full, picks_taken = (
            sem(n) for n in ("gexp_in", "gexp_done", "picks_done", "picks_full", "picks_taken"))
        oh_ready, g_full, g_evac = sem("oh_ready"), sem("g_full"), sem("g_evac")
        g_stored = [sem(f"g_stored{w}") for w in range(2)]
        g4_in, gelu_done, w_prod, wwh_done, w_ready, part_done, out_evac = (
            sem(n) for n in ("g4_in", "gelu_done", "w_prod", "wwh_done", "w_ready", "part_done", "out_evac"))
        dve_own = sem("dve_own")
        dve_apart, pool_apart = sem("dve_apart"), sem("pool_apart")

        STEPS = [(hh, i) for hh in range(2) for i in range(4)] + [(0, "sample"), (1, "sample")]
        NS = len(STEPS)

        def width(mix, i):
            if i == "sample":
                return 2 * P
            return P * (i + 1) if mix == "a" else P * min(i + 1, 2)

        T_USES = {m: ([("v", 0), ("v", 1)] if m == "a" else [])
                  + [("t", t) for t in range(6)] + [("c", 0), ("t", 6), ("c", 1)] + [("t", t) for t in range(7, NS)]
                  for m in "ab"}
        T_BASE = {"a": 0, "b": len(T_USES["a"]) * PAIRS + 2}
        STEP_BASE = {"a": 0, "b": NS * PAIRS}
        IN_BASE = {"a": 0, "b": 16 * (7 * PAIRS + 4)}
        IN_PER = {"a": 16 * 7, "b": 16 * 3}

        def t_use(mix, j, what, extra=0):
            return T_BASE[mix] + j * len(T_USES[mix]) + T_USES[mix].index(what) + extra

        block = ctx.enter_context(nc.Block())

        @block.sync
        def _(sp):
            for s in range(2):
                sp.dma_start(raw[s][:, :], wstream[s]).then_inc(raw_full[s], 16)
            with sp.Fori(1, UNITS // 2) as i:
                for s in range(2):
                    sp.wait_ge(split_done, 2 * i + s - 1)
                    sp.dma_start(raw[s][:, :], wstream[ds(2 * i + s, 1)].rearrange("a p c -> p (a c)")) \
                        .then_inc(raw_full[s], 16)

        @block.gpsimd
        def _(pool):
            def split(s, pair):
                pool.wait_ge(raw_full[s], 16 * pair + 16)
                pool.sem_inc(pool_apart, 1)
                pool.tensor_scalar(w_hi[s][:, :], raw[s][:, :], 1.0, 0.0, ALU.mult, ALU.add).then_inc(hi_done, 1)
                pool.wait_ge(hi_done, 2 * pair + s + 1)
                pool.tensor_tensor(w_lo[s][:, :], raw[s][:, :], w_hi[s][:, :].bitcast(f32), ALU.subtract) \
                    .then_inc(split_done, 1)

            for s in range(2):
                split(s, 0)
            with pool.Fori(1, UNITS // 2) as i:
                for s in range(2):
                    pool.wait_ge(unit_done, 2 * i + s - 1)
                    split(s, i)

        @block.tensor
        def _(pe):
            def k_step(s, k, dst, k_first, k_last, phase):
                if phase is not None and k % 4 == 0:
                    pe.wait_ge(mv_ready, KT_N * phase + k + 4)
                for n, (a, b) in enumerate(((w_hi, mv_hi), (w_hi, mv_lo), (w_lo, mv_hi))):
                    for h in range(2):
                        last = pe.matmul(acc(dst)[:, h, :], a[s][:, P * k:P * k + P], b[:, k, HALF * h:HALF * h + HALF],
                                         start=(k == k_first and n == 0), stop=(k == k_last and n == 2))
                return last

            def unit(s, n, free, phase):
                pe.wait_ge(split_done, n + 1)
                pe.wait_ge(*free)
                for k in range(KT_N):
                    last = k_step(s, k, s, 0, KT_N - 1, phase)
                last.then_inc(unit_done, 1)

            with pe.Fori(0, N_QKV // 2) as i:
                for s in range(2):
                    unit(s, U_QKV + 2 * i + s, (qkv_evac, 2 * i + s + 1), 0)

            def scores(mix, j, t):
                hh, i = STEPS[t]
                rows = slice(HD * hh, HD * hh + HD)
                bank = s_bank[t % 2]
                if t >= 1:
                    pe.wait_ge(s_taken, STEP_BASE[mix] + NS * j + t - 1)
                if i == "sample":
                    pe.wait_ge(t_taken, t_use(mix, j, ("c", hh), 1))
                    pe.transpose(bank[:, 0:P], st_sb[hh][:, :], ident)
                    last = pe.matmul(bank[:, P:2 * P], q_t[rows, SEQ:T], k_t[rows, SEQ:T], start=True, stop=True)
                else:
                    w = width(mix, i)
                    end = P * (i + 1)
                    last = pe.matmul(bank[:, 0:w], q_t[rows, P * i:end], k_t[rows, end - w:end], start=True, stop=True)
                last.then_inc(s_full, 1)

            def transpose_p(mix, j, t):
                w = width(mix, STEPS[t][1])
                pe.wait_ge(p_ready, STEP_BASE[mix] + NS * j + t + 1)
                pe.wait_ge(t_taken, t_use(mix, j, ("t", t)))
                for c in range(w // P):
                    last = pe.transpose(t_bank[:, P * c:P * c + P], s_sb[t % 2][:, P * c:P * c + P], ident)
                last.then_inc(t_full, 1)

            def cached_scores(mix, j, hh):
                rows = slice(HD * hh, HD * hh + HD)
                pe.wait_ge(t_taken, t_use(mix, j, ("c", hh)))
                for b in range(DEC_B):
                    c = DEC_T * b
                    last = pe.matmul(t_bank[:, c:c + DEC_T], ck_t[rows, P * b:P * b + P],
                                     q_t[rows, SEQ + c:SEQ + c + DEC_T], start=True, stop=True)
                last.then_inc(t_full, 1)

            def values(mix, j, t):
                hh, i = STEPS[t]
                rows, pt = slice(HD * hh, HD * hh + HD), pt_sb[t % 2]
                pe.wait_ge(t_taken, t_use(mix, j, ("t", t), 1))
                pe.wait_ge(o_taken, STEP_BASE[mix] + NS * j + t)
                o = o_bank[rows, 0:P]
                if i == "sample":
                    for b in range(DEC_B):
                        c = DEC_T * b
                        pe.matmul(o[:, c:c + DEC_T], cv_t[:, P * b + HD * hh:P * b + HD * hh + HD],
                                  pt[:, c:c + DEC_T], start=(b == 0), stop=False)
                    last = pe.matmul(o, vn[:, P * 4 + HD * hh:P * 4 + HD * hh + HD], pt[:, P:2 * P],
                                     start=False, stop=True)
                else:
                    nk = width(mix, i) // P
                    for c in range(nk):
                        kb = i + 1 - nk + c
                        last = pe.matmul(o, vn[:, P * kb + HD * hh:P * kb + HD * hh + HD], pt[:, P * c:P * c + P],
                                         start=(c == 0), stop=(c == nk - 1))
                last.then_inc(o_full, 1)

            def transpose_v(first, use):
                pe.wait_ge(t_taken, use)
                for b in (range(4) if first else (4,)):
                    last = pe.transpose(t_bank[:, P * (b % 4):P * (b % 4) + P], v_t[:, P * b:P * b + P], ident)
                last.then_inc(t_full, 1)

            def attention_pair(mix, j):
                first = U_GATE + 2 * (j + (PAIRS if mix == "b" else 0))
                k_steps = [(s, k) for s in range(2) for k in range(KT_N)]

                def gemm(n):
                    for _ in range(n):
                        s, k = k_steps.pop(0)
                        if k == 0:
                            pe.wait_ge(split_done, first + s + 1)
                            pe.wait_ge(gate_evac, first - U_GATE + s + 1)
                        last = k_step(s, k, s, 0, KT_N - 1, None)
                        if k == KT_N - 1:
                            last.then_inc(unit_done, 1)

                gemm(10)
                pe.wait_ge(att_in, IN_BASE[mix] + IN_PER[mix] * j + IN_PER[mix])
                if mix == "a":
                    transpose_v(True, t_use(mix, j, ("v", 0)))
                gemm(2)
                if mix == "a":
                    transpose_v(False, t_use(mix, j, ("v", 1)))
                for t in range(NS + 2):
                    if t < NS:
                        scores(mix, j, t)
                    if k_steps:
                        gemm(2)
                    if 1 <= t <= NS:
                        transpose_p(mix, j, t - 1)
                    if t >= 2:
                        values(mix, j, t - 2)
                    if t in (6, 7):
                        cached_scores(mix, j, t - 6)
                assert not k_steps

            pe.wait_ge(const_in, 64)
            with pe.Fori(0, PAIRS) as j:
                attention_pair("a", j)
            pe.wait_ge(att_in, IN_BASE["b"])
            transpose_v(True, T_BASE["b"] - 2)
            transpose_v(False, T_BASE["b"] - 1)
            with pe.Fori(0, PAIRS) as j:
                attention_pair("b", j)

            with pe.Fori(0, N_PROJ // 2) as i:
                for s in range(2):
                    m = 2 * i + s
                    pe.wait_ge(split_done, U_PROJ + m + 1)
                    for z in range(2):
                        pe.wait_ge(z_taken, 2 * m + z + 1)
                        for k in range(8 * z, 8 * z + 8):
                            last = k_step(s, k, z, 8 * z, 8 * z + 7, 1)
                        last.then_inc((za_done, unit_done)[z], 1)

            with pe.Fori(0, N_OUT // 2) as i:
                for s in range(2):
                    unit(s, U_OUT + 2 * i + s, (r_done, 2 * i + s + 1), 2)

            def layer_norm(q, ready):
                pe.wait_ge(*ready)
                for k in range(KT_N):
                    for h in range(2):
                        last = pe.matmul(acc(0)[:, h, :], ones, Rt[:, k, HALF * h:HALF * h + HALF],
                                         start=(k == 0), stop=(k == KT_N - 1))
                last.then_inc(ln[q]["sum"], 1)
                for k in range(KT_N):
                    pe.wait_ge(ln[q]["squared"], k + 1)
                    for h in range(2):
                        last = pe.matmul(acc(1)[:, h, :], ones, sq_t[k % 2][:, HALF * h:HALF * h + HALF],
                                         start=(k == 0), stop=(k == KT_N - 1))
                    last.then_inc(ln[q]["sq_used"], 1)

            layer_norm(0, (r_done, N_OUT + 2))

            def key_scores(s, c):
                pe.wait_ge(q_evac, c + 3)
                pe.wait_ge(sc_taken, c + 1)
                four, one = sc_parts(s)
                for b in range(NB):
                    out = four[:, P * b:P * b + P] if b < 4 else one
                    last = pe.matmul(out, qe[s][:, P * b:P * b + P], subkt[:, KEYS * s:KEYS * s + KEYS],
                                     start=True, stop=True)
                last.then_inc(sc_full, 1)

            with pe.Fori(0, N_QUERY // 2) as i:
                unit(0, U_QUERY + 2 * i, (q_evac, 2 * i + 1), 3)
                pe.wait_ge(split_done, U_QUERY + 2 * i + 2)
                pe.wait_ge(q_evac, 2 * i + 2)
                for k in range(KT_N):
                    last = k_step(1, k, 1, 0, KT_N - 1, 3)
                    if k == 3:
                        key_scores(0, 2 * i)
                last.then_inc(unit_done, 1)
                key_scores(1, 2 * i + 1)

            pe.wait_ge(sc_taken, 2 + N_QUERY)
            pe.wait_ge(q_evac, 2 + N_QUERY)
            pe.wait_ge(picks_done, 1)
            for q, src in enumerate((pick_g, pick_e[0], pick_e[1])):
                four, one = sc_parts(q) if q < 2 else (banks[:, 0, :], banks[:, 1, 0:P])
                for b in range(NB):
                    last = pe.transpose(four[:, P * b:P * b + P] if b < 4 else one, src[:, b, :], ident)
                last.then_inc(picks_full, 1)

            pe.wait_ge(picks_taken, 3)
            pe.sem_inc(g_full, 2)
            with pe.Fori(0, GBLK // 2) as i:
                for q in range(2 * GT // 4):
                    pe.wait_ge(oh_ready, 20 * i + q + 1)
                    pe.wait_ge(g_evac, 20 * i + q + 1)
                    for t in range(4):
                        n = 4 * (q % 2) + t
                        last = pe.matmul(banks[:, q % 4, P * t:P * t + P], oh2[:, n, :].bitcast(f32), oh1[:, n, :],
                                         start=True, stop=True)
                    last.then_inc(g_full, 1)
            pe.wait_ge(g_evac, 4 + T // 4)

            with pe.Fori(0, GROUPS) as g:
                for e in range(EG):
                    free = ((out_evac, 16 * g), (out_evac, 16 * g + 1), (gelu_done, 4 * g + 1), (gelu_done, 4 * g + 2))[e]
                    unit(e % 2, U_PEER + 8 * g + e, free, None)
                for v in range(EG):
                    s = v % 2
                    pe.wait_ge(split_done, U_PEER + 8 * g + EG + v + 1)
                    for d in range(4):
                        dt = 4 * v + d
                        if dt < 2:
                            pe.wait_ge(gelu_done, 4 * g + 3 + dt)
                        else:
                            pe.wait_ge(out_evac, 16 * g + dt)
                        for e in range(EG):
                            if dt == 0:
                                pe.wait_ge(w_ready, 4 * g + e + 3)
                            for n, (a, b) in enumerate(((w_hi, ww_hi), (w_hi, ww_lo), (w_lo, ww_hi))):
                                for h in range(2):
                                    at = P * (EG * d + e)
                                    last = pe.matmul(acc(dt % 2)[:, h, :], a[s][:, at:at + P],
                                                     b[:, e, HALF * h:HALF * h + HALF],
                                                     start=(e == 0 and n == 0), stop=(e == EG - 1 and n == 2))
                        last.then_inc(unit_done if d == 3 else part_done, 1)

            layer_norm(1, (res_done, KT_N))

        @block.scalar
        def _(act):
            act.dma_start(cst[:, :], consts).then_inc(const_in, 16)
            act.dma_start(subkt[:, :], subk).then_inc(const_in, 16)
            act.dma_start(sinkt[:, :], sinks).then_inc(const_in, 16)
            act.dma_start(lnt[:, :], lnp).then_inc(const_in, 16)

            def load_moving(src, phase, after):
                for w in after:
                    act.wait_ge(*w)
                for q in range(4):
                    act.dma_start(Rt[:, 4 * q:4 * q + 4, :], src[4 * q:4 * q + 4].rearrange("k p t -> p k t")) \
                        .then_inc(mv_in[q], 16)
                for k in range(KT_N):
                    if k % 4 == 0:
                        act.wait_ge(mv_in[k // 4], 16 * phase + 16)
                    act.activation(mv_hi[:, k, :], Rt[:, k, :], ACT.Copy).then_inc(mvh_done, 1)

            load_moving(x_t, 0, ())

            rt = rext.tensor
            n_r = rext.shape[1]
            act.dma_start(bp_a[:, 64:P, :], bass.AP(rt, 63, [[n_r, 16], [-1, 64], [1, 512]])).then_inc(tab_done, 16)
            act.dma_start(bp_a[:, 0:64, 0:448], bass.AP(rt, 127, [[n_r, 16], [-1, 64], [1, 448]])).then_inc(tab_done, 16)
            act.dma_start(bp_a[:, 0:64, 448:512], negs).then_inc(tab_done, 16)
            for b in range(DEC_B):
                act.dma_start(bs_a[:, DEC_T * b:DEC_T * b + DEC_T, :], bass.AP(rt, 383, [[n_r, 16], [-1, 16], [1, 144]])) \
                    .then_inc(tab_done, 16)

            act.sem_inc(qkv_evac, 2)
            with act.Fori(0, N_QKV // 2) as i:
                for s in range(2):
                    act.wait_ge(unit_done, 2 * i + s + 1)
                    act.wait_ge(qkv_stored[s], 16 * i)
                    act.activation(two(ev[s]), acc(s), ACT.Copy).then_inc(qkv_evac, 1)
                    act.wait_ge(qkv_evac, 2 * i + s + 3)
                    act.dma_start(pt_out[ds(2 * i + s, 1)].rearrange("a p t -> p (a t)"), ev[s]) \
                        .then_inc(qkv_stored[s], 16)

            def gate_evacuate(n, s, trip):
                act.wait_ge(unit_done, U_GATE + n + 1)
                act.wait_ge(gate_stored[s], 16 * trip)
                act.activation(two(ev[s]), acc(s), ACT.Copy).then_inc(gate_evac, 1)
                act.wait_ge(gate_evac, n + 3)
                act.dma_start(g_s[ds(n, 1)].rearrange("a p t -> p (a t)"), ev[s]).then_inc(gate_stored[s], 16)

            def take(mix, j, what):
                kind, t = what
                if kind == "v":
                    src, dst = (t_bank[:, 0:512], vn[:, 0:512]) if t == 0 else (t_bank[:, 0:P], vn[:, 512:T])
                elif kind == "c":
                    src, dst = t_bank[:, 0:P], st_sb[t][:, :]
                else:
                    w = width(mix, STEPS[t][1])
                    src, dst = t_bank[:, 0:w], pt_sb[t % 2][:, 0:w]
                    if t >= 2:
                        act.wait_ge(o_full, STEP_BASE[mix] + NS * j + t - 1)
                act.wait_ge(t_full, t_use(mix, j, what, 1))
                act.activation(dst, src, ACT.Copy).then_inc(t_taken, 1)

            def attention_pair(mix, j, pair):
                def load(dst, src):
                    act.dma_start(dst, src).then_inc(att_in, 16)

                def row(src, r):
                    return src[ds(r, 1)].rearrange("a p t -> p (a t)")

                if mix == "a":
                    load(q_t, row(pt_out, ROW_QA + j))
                    load(k_t, row(pt_out, j))
                    load(v_t, row(pt_out, 8 + j))
                    load(ck_t, row(cka, j))
                    load(cv_t, row(cva, j))
                    load(bp_t, bp_a[ds(2 * j, 2)].rearrange("h p c -> p h c"))
                    load(bs_t, bs_a[ds(2 * j, 2)].rearrange("h p c -> p h c"))
                else:
                    load(q_t, row(pt_out, ROW_QB + j))
                    load(bp_t[:, :, 256:512], bp_b[ds(2 * j, 2)].rearrange("h p c -> p h c"))
                    load(bs_t, bs_b[ds(2 * j, 2)].rearrange("h p c -> p h c"))
                if mix == "a":
                    take(mix, j, ("v", 0))
                    take(mix, j, ("v", 1))
                for t in range(NS + 1):
                    if t < NS:
                        w, step = width(mix, STEPS[t][1]), STEP_BASE[mix] + NS * j + t
                        act.wait_ge(nmax_ready, step + 1)
                        exp = act.activation(s_sb[t % 2][:, 0:w], s_sb[t % 2][:, 0:w], ACT.Exp, bias=nmax[t % 2],
                                             accum_out=rsum[t % 2])
                        if mix == "b":
                            col = 2 * j + STEPS[t][0]
                            exp = act.activation(esink[t % 2], sinkt[:, ds(col, 1)], ACT.Exp, bias=nmax[t % 2])
                        exp.then_inc(e_ready, 1)
                    if t >= 1:
                        take(mix, j, ("t", t - 1))
                    if t in (6, 7):
                        take(mix, j, ("c", t - 6))
                    if t == 4:
                        gate_evacuate(2 * pair, 0, pair)
                act.wait_ge(o_taken, STEP_BASE[mix] + NS * j + NS)
                act.dma_start(y_s[ds(pair, 1)].rearrange("a p t -> p (a t)"), y_t).then_inc(y_stored, 16)
                gate_evacuate(2 * pair + 1, 1, pair)

            act.sem_inc(gate_evac, 2)
            for s in range(2):
                act.wait_ge(qkv_stored[s], 16 * (N_QKV // 2))
            act.wait_ge(tab_done, 16 * (3 + DEC_B))
            act.wait_ge(mv_ready, KT_N)
            with act.Fori(0, PAIRS) as j:
                attention_pair("a", j, j)
            for dst, src in ((k_t, pt_out[ROW_KB]), (v_t, pt_out[ROW_KB + 1]), (ck_t, ckb), (cv_t, cvb)):
                act.dma_start(dst, src).then_inc(att_in, 16)
            for n in range(2):
                act.wait_ge(t_full, T_BASE["b"] - 1 + n)
                src, dst = (t_bank[:, 0:512], vn[:, 0:512]) if n == 0 else (t_bank[:, 0:P], vn[:, 512:T])
                act.activation(dst, src, ACT.Copy).then_inc(t_taken, 1)
            with act.Fori(0, PAIRS) as j:
                attention_pair("b", j, PAIRS + j)

            load_moving(y_s, 1, ((y_stored, 16 * 2 * PAIRS), (unit_done, U_PROJ)))
            for s in range(2):
                act.wait_ge(gate_stored[s], 16 * 2 * PAIRS)
            with act.Fori(0, N_PROJ // 2) as i:
                for s in range(2):
                    m = 2 * i + s
                    act.wait_ge(msum_done, m + 1)
                    act.dma_start(gate_t[s].rearrange("p (a t) -> p a t", a=2),
                                  g_s[ds(2 * m, 2)].rearrange("a p t -> p a t")).then_inc(gate_in[s], 16)
                    act.wait_ge(gate_in[s], 16 * i + 16)
                    act.activation(gate_t[s], gate_t[s], ACT.Sigmoid).then_inc(sig_done, 1)
                    act.wait_ge(msum_done, m + 3)
                    act.dma_start(m_s[ds(m, 1)].rearrange("a p t -> p (a t)"), ev[s]).then_inc(m_stored[s], 16)

            load_moving(m_s, 2, ((m_stored[0], 16 * (N_PROJ // 2)), (m_stored[1], 16 * (N_PROJ // 2)), (unit_done, U_OUT)))
            with act.Fori(0, N_OUT // 2) as i:
                for s in range(2):
                    act.wait_ge(r_done, 2 * i + s + 1)
                    act.dma_start(x_res[s], x_t[ds(2 * i + s, 1)].rearrange("a p t -> p (a t)")).then_inc(x_in[s], 16)

            def layer_norm(q, finish):
                for k in range(KT_N):
                    act.wait_ge(ln[q]["centered"], k + 1)
                    if k >= 2:
                        act.wait_ge(ln[q]["sq_used"], k - 1)
                    act.activation(sq_t[k % 2], Rt[:, k, :], ACT.Square).then_inc(ln[q]["squared"], 1)
                act.wait_ge(ln[q]["var"], 1)
                act.activation(rstd_t, rstd_t, ACT.Sqrt).then_inc(ln[q]["std"], 1)
                for k in range(KT_N):
                    act.wait_ge(ln[q]["scaled"], k + 1)
                    act.activation(Rt[:, k, :], Rt[:, k, :], ACT.Identity, bias=lnt[:, 2 * KT_N * q + KT_N + k:][:, 0:1],
                                   scale=lnt[:, 2 * KT_N * q + k:][:, 0:1]).then_inc(ln[q]["out"], 1)
                    act.wait_ge(ln[q]["out"], k + 1)
                    finish(k)

            act.wait_ge(const_in, 64)
            layer_norm(0, lambda k: act.activation(mv_hi[:, k, :], Rt[:, k, :], ACT.Copy).then_inc(mvh_done, 1))

            act.wait_ge(mv_ready, 4 * KT_N)
            act.sem_inc(q_evac, 2)
            act.sem_inc(sc_taken, 2)
            with act.Fori(0, N_QUERY // 2) as i:
                for s in range(2):
                    c = 2 * i + s
                    act.wait_ge(unit_done, U_QUERY + c + 1)
                    act.activation(two(qe[s]), acc(s), ACT.Copy).then_inc(q_evac, 1)
                    act.wait_ge(sc_full, c + 1)
                    act.wait_ge(topk_done, c + 1)
                    four, one = sc_parts(s)
                    act.activation(sc_sb[s][:, 0:512], four, ACT.Copy)
                    act.activation(sc_sb[s][:, 512:T], one, ACT.Copy).then_inc(sc_taken, 1)

            act.wait_ge(gexp_in, 1)
            flat = pick_g.rearrange("p b k -> p (b k)")
            act.activation(flat, flat, ACT.Exp).then_inc(gexp_done, 1)
            for q in range(3):
                act.wait_ge(picks_full, q + 1)
                four, one = sc_parts(q) if q < 2 else (banks[:, 0, :], banks[:, 1, 0:P])
                act.activation(pick_t[q][:, 0:512], four, ACT.Copy)
                act.activation(pick_t[q][:, 512:T], one, ACT.Copy).then_inc(picks_taken, 1)

            act.sem_inc(g_evac, 4)
            with act.Fori(0, GBLK // 2) as i:
                for q in range(2 * GT // 4):
                    w, qq = q // 10, q % 10
                    act.wait_ge(g_full, 20 * i + q + 3)
                    if qq == 0:
                        act.wait_ge(g_stored[w], 16 * i)
                    act.activation(g_buf[w][:, :, 4 * qq:4 * qq + 4],
                                   banks[:, q % 4, :].rearrange("p (t e) -> p e t", t=4), ACT.Copy).then_inc(g_evac, 1)
                    if qq == 9:
                        act.wait_ge(g_evac, 20 * i + q + 5)
                        act.dma_start(G_s[ds(2 * i + w, 1)].rearrange("a p e t -> p (a e t)"),
                                      g_buf[w].rearrange("p e t -> p (e t)")).then_inc(g_stored[w], 16)

            for w in range(2):
                act.wait_ge(g_stored[w], 16 * (GBLK // 2))
            with act.Fori(0, GROUPS) as g:
                act.wait_ge(w_prod, 4 * g)
                act.dma_start(G4.rearrange("p b e t -> p b (e t)"),
                              G_s[:, :, ds(EG * g, EG), :].rearrange("b p e t -> p b (e t)")).then_inc(g4_in, 16)
                for e in range(EG):
                    act.wait_ge(unit_done, U_PEER + 8 * g + e + 1)
                    act.wait_ge(w_ready, 4 * g + e + 1)
                    act.activation(two(act_t[e % 2]), acc(e % 2), ACT.Gelu).then_inc(gelu_done, 1)
                    act.wait_ge(w_prod, 4 * g + e + 1)
                    act.activation(ww_hi[:, e, :], act_t[e % 2], ACT.Copy).then_inc(wwh_done, 1)

            layer_norm(1, lambda k: act.dma_start(y_out[k], Rt[:, k, :]).then_inc(y_out_done, 16))
            act.wait_ge(y_out_done, 16 * KT_N)

        @block.vector
        def _(dve):
            own = Own(dve, dve_own, dve_apart)

            def split_low(phase):
                for k in range(KT_N):
                    dve.wait_ge(mvh_done, KT_N * phase + k + 1)
                    dve.tensor_tensor(mv_lo[:, k, :], Rt[:, k, :], mv_hi[:, k, :].bitcast(f32), ALU.subtract) \
                        .then_inc(mv_ready, 1)

            dve.wait_ge(mv_in[0], 16)
            split_low(0)

            def soft_in(mix, j, t):
                hh, i = STEPS[t]
                w, step = width(mix, i), STEP_BASE[mix] + NS * j + t
                buf, bank = s_sb[t % 2], s_bank[t % 2]
                dve.wait_ge(s_full, step + 1)
                if t >= 2:
                    dve.wait_ge(t_full, t_use(mix, j, ("t", t - 2), 1))
                if i == "sample":
                    dve.scalar_tensor_tensor(buf[:, 0:P], bank[:, 0:P], SCALE, bs_t[:, hh, 0:P], ALU.mult, ALU.add)
                    dve.scalar_tensor_tensor(buf[:, P:2 * P], bank[:, P:2 * P], SCALE, bmask, ALU.mult, ALU.add) \
                        .then_inc(s_taken, 1)
                    dve.wait_ge(s_taken, step + 1)
                    new = buf[:, P:2 * P].rearrange("p (b t) -> p b t", b=DEC_B)
                    own.done(dve.tensor_tensor(new, new, bs_t[:, hh, P:P + DEC_T].unsqueeze(1)
                                               .to_broadcast([P, DEC_B, DEC_T]), ALU.add))
                    own.wait()
                else:
                    dve.scalar_tensor_tensor(buf[:, 0:w], bank[:, 0:w], SCALE, bp_t[:, hh, 512 - P * (w // P):512]
                                             if mix == "b" else bp_t[:, hh, 384 - P * i:512], ALU.mult, ALU.add) \
                        .then_inc(s_taken, 1)
                    dve.wait_ge(s_taken, step + 1)
                if mix == "a":
                    dve.tensor_reduce(nmax[t % 2], buf[:, 0:w], AX.X, ALU.max, negate=True).then_inc(nmax_ready, 1)
                else:
                    own.done(dve.tensor_reduce(mx[t % 2], buf[:, 0:w], AX.X, ALU.max))
                    own.wait()
                    dve.tensor_scalar(nmax[t % 2], mx[t % 2], sinkt[:, ds(2 * j + hh, 1)], -1.0, ALU.max, ALU.mult) \
                        .then_inc(nmax_ready, 1)

            def soft_out(mix, j, t):
                w = width(mix, STEPS[t][1])
                dve.wait_ge(e_ready, STEP_BASE[mix] + NS * j + t + 1)
                total = rsum[t % 2]
                if mix == "b":
                    own.done(dve.tensor_tensor(den[t % 2], rsum[t % 2], esink[t % 2], ALU.add))
                    own.wait()
                    total = den[t % 2]
                own.done(dve.reciprocal(rden[t % 2], total))
                own.wait()
                dve.tensor_scalar(s_sb[t % 2][:, 0:w], s_sb[t % 2][:, 0:w], rden[t % 2], None, ALU.mult) \
                    .then_inc(p_ready, 1)

            def out_take(mix, j, t, pair):
                hh, i = STEPS[t]
                rows, at = slice(HD * hh, HD * hh + HD), SEQ if i == "sample" else P * i
                if t == 0:
                    dve.wait_ge(y_stored, 16 * pair)
                dve.wait_ge(o_full, STEP_BASE[mix] + NS * j + t + 1)
                dve.tensor_copy(y_t[rows, at:at + P], o_bank[rows, 0:P]).then_inc(o_taken, 1)

            dve.wait_ge(const_in, 64)
            for mix in "ab":
                with dve.Fori(0, PAIRS) as j:
                    own.enter(j, 2 + NS * (1 if mix == "a" else 3))
                    dve.wait_ge(att_in, IN_BASE[mix] + IN_PER[mix] * j + IN_PER[mix])
                    for t in range(NS + 2):
                        if t < NS:
                            soft_in(mix, j, t)
                        if 1 <= t <= NS:
                            soft_out(mix, j, t - 1)
                        if t >= 2:
                            out_take(mix, j, t - 2, j + (PAIRS if mix == "b" else 0))
                    own.leave(PAIRS)

            split_low(1)
            dve.sem_inc(z_taken, 2)
            dve.sem_inc(msum_done, 2)
            with dve.Fori(0, N_PROJ // 2) as i:
                for s in range(2):
                    m = 2 * i + s
                    ga, gb = gate_t[s][:, 0:T], gate_t[s][:, T:2 * T]
                    dve.wait_ge(sig_done, m + 1)
                    dve.wait_ge(za_done, m + 1)
                    dve.tensor_tensor(two(ga), acc(0), two(ga), ALU.mult).then_inc(z_taken, 1)
                    dve.wait_ge(unit_done, U_PROJ + m + 1)
                    dve.tensor_tensor(two(gb), acc(1), two(gb), ALU.mult).then_inc(z_taken, 1)
                    dve.wait_ge(z_taken, 2 * m + 4)
                    dve.wait_ge(m_stored[s], 16 * i)
                    dve.tensor_tensor(ev[s], ga, gb, ALU.add).then_inc(msum_done, 1)

            split_low(2)
            dve.sem_inc(r_done, 2)
            with dve.Fori(0, N_OUT // 2) as i:
                for s in range(2):
                    m = 2 * i + s
                    dve.wait_ge(x_in[s], 16 * i + 16)
                    dve.wait_ge(unit_done, U_OUT + m + 1)
                    dve.scalar_tensor_tensor(two(R[:, ds(T * m, T)]), two(x_res[s]), ALPHA, acc(s), ALU.mult, ALU.add) \
                        .then_inc(r_done, 1)

            def layer_norm(q):
                dve.wait_ge(ln[q]["sum"], 1)
                own.done(dve.tensor_scalar(two(mean_t), acc(0), 1.0 / D, None, ALU.mult))
                own.wait()
                for k in range(KT_N):
                    dve.tensor_tensor(Rt[:, k, :], Rt[:, k, :], mean_t, ALU.subtract).then_inc(ln[q]["centered"], 1)
                dve.wait_ge(ln[q]["sq_used"], KT_N)
                dve.tensor_scalar(two(rstd_t), acc(1), 1.0 / D, EPS, ALU.mult, ALU.add).then_inc(ln[q]["var"], 1)
                dve.wait_ge(ln[q]["std"], 1)
                own.done(dve.reciprocal(rstd_t, rstd_t))
                own.wait()
                dve.wait_ge(ln[q]["centered"], KT_N)
                for k in range(KT_N):
                    dve.tensor_tensor(Rt[:, k, :], Rt[:, k, :], rstd_t, ALU.mult).then_inc(ln[q]["scaled"], 1)

            layer_norm(0)
            split_low(3)

            def top16(n, src, alt, out_v, out_i):
                for b in range(NB):
                    last = dve.max(out_v(b)[:, 0:8], src(b))
                own.done(last)
                own.wait_apart()
                for b in range(NB):
                    dve.max_index(out_i(b)[:, 0:8], out_v(b)[:, 0:8], src(b))
                    last = dve.match_replace(alt(b), out_v(b)[:, 0:8], src(b), -3e38)
                own.done(last)
                own.wait_apart()
                for b in range(NB):
                    last = dve.max(out_v(b)[:, 8:16], alt(b))
                own.done(last)
                own.wait_apart()
                for b in range(NB):
                    last = dve.max_index(out_i(b)[:, 8:16], out_v(b)[:, 8:16], alt(b))
                return last

            dve.sem_inc(topk_done, 2)
            cand4 = cand.rearrange("p (b i j) -> p b i j", b=NB, i=TOPK)
            eq3 = eq.rearrange("p (n k) -> p n k", k=TOPK)
            eq4 = eq.rearrange("p (b n k) -> p b n k", b=NB, n=TOPK)
            full = [P, NB, TOPK, TOPK]
            with dve.Fori(0, N_QUERY // 2) as i:
                own.enter(i, 6 + 1 + 3 + 1 + 2 + 6)
                for s in range(2):
                    dve.wait_ge(sc_taken, 2 * i + s + 3)
                    dve.sem_inc(dve_apart, 1)
                    top16(KEYS, lambda b: sc_sb[s][:, P * b:P * b + P], lambda b: sc2[:, P * b:P * b + P],
                          lambda b: val[:, b, s, :], lambda b: idx_u[:, b, s, :]).then_inc(topk_done, 1)
                dve.wait_ge(topk_done, 2 * i + 4)
                dve.tensor_copy(idx_f, idx_u)
                own.done(dve.tensor_tensor(cand4, val[:, :, 0, :].unsqueeze(3).to_broadcast(full),
                                           val[:, :, 1, :].unsqueeze(2).to_broadcast(full), ALU.add))
                own.wait_apart()
                own.done(top16(TOPK * TOPK, lambda b: cand[:, 256 * b:256 * b + 256], lambda b: cand2[:, 256 * b:256 * b + 256],
                               lambda b: top_v[:, TOPK * b:TOPK * b + TOPK], lambda b: ci_u[:, TOPK * b:TOPK * b + TOPK]))
                own.wait()
                dve.tensor_copy(pick_g[:, :, ds(TOPK * i, TOPK)], top_v.rearrange("p (b k) -> p b k", b=NB))
                dve.tensor_scalar(cp_u[0], ci_u, 4, None, ALU.logical_shift_right)
                own.done(dve.tensor_scalar(cp_u[1], ci_u, TOPK - 1, None, ALU.bitwise_and))
                own.wait()
                dve.tensor_copy(c_f[0], cp_u[0])
                own.done(dve.tensor_copy(c_f[1], cp_u[1]))
                own.wait()
                for z in range(2):
                    own.done(dve.tensor_tensor(eq3, c_f[z].unsqueeze(2).to_broadcast([P, NB * TOPK, TOPK]),
                                               iota[:, 0:TOPK].unsqueeze(1).to_broadcast([P, NB * TOPK, TOPK]),
                                               ALU.is_equal))
                    own.wait()
                    own.done(dve.tensor_tensor(eq4, eq4, idx_f[:, :, z, :].unsqueeze(2).to_broadcast(full), ALU.mult))
                    own.wait()
                    own.done(dve.tensor_reduce(pick_e[z][:, :, ds(TOPK * i, TOPK)], eq4, AX.X, ALU.add))
                    own.wait()
                own.leave(N_QUERY // 2)

            g3 = pick_g.rearrange("p b (h k) -> p (b h) k", k=TOPK)
            own.wait()
            gm = cand[:, 0:NB * PH]
            own.done(dve.tensor_copy(gm.unsqueeze(2), g3[:, :, 0:1]))
            own.wait()
            wide = [P, NB * PH, TOPK]
            dve.tensor_tensor(g3, g3, gm.unsqueeze(2).to_broadcast(wide), ALU.subtract).then_inc(gexp_in, 1)
            dve.wait_ge(gexp_done, 1)
            own.done(dve.tensor_reduce(psum_g, g3, AX.X, ALU.add))
            own.wait()
            own.done(dve.reciprocal(psum_g, psum_g))
            own.wait()
            dve.tensor_tensor(g3, g3, psum_g.unsqueeze(2).to_broadcast(wide), ALU.mult).then_inc(picks_done, 1)

            dve.wait_ge(picks_taken, 3)
            with dve.Fori(0, GBLK // 2) as i:
                for q in range(2 * GT // 4):
                    dve.wait_ge(g_full, 20 * i + q + 1)
                    for t in range(4):
                        n = 4 * (q % 2) + t
                        tok = ds(2 * GT * i + 4 * q + t, 1)
                        dve.tensor_scalar(oh2[:, n, :], iota, pick_t[2][:, tok], None, ALU.is_equal)
                        last = dve.tensor_scalar(oh1[:, n, :], iota, pick_t[1][:, tok], pick_t[0][:, tok],
                                                 ALU.is_equal, ALU.mult)
                    last.then_inc(oh_ready, 1)

            for w in range(2):
                dve.wait_ge(g_stored[w], 16 * (GBLK // 2))
            dve.memset(R[:, :], 0.0).then_inc(out_evac, 1)
            dve.wait_ge(out_evac, 1)
            dve.sem_inc(w_ready, 2)
            with dve.Fori(0, GROUPS) as g:
                dve.wait_ge(g4_in, 16 * g + 16)
                for e in range(EG):
                    dve.wait_ge(gelu_done, 4 * g + e + 1)
                    a3 = act_t[e % 2].rearrange("p (b t) -> p b t", b=GBLK)
                    dve.tensor_tensor(a3, a3, G4[:, :, e, :], ALU.mult).then_inc(w_prod, 1)
                    dve.wait_ge(wwh_done, 4 * g + e + 1)
                    dve.tensor_tensor(ww_lo[:, e, :], act_t[e % 2], ww_hi[:, e, :].bitcast(f32), ALU.subtract) \
                        .then_inc(w_ready, 1)
                for dt in range(KT_N):
                    v, d = dt // 4, dt % 4
                    if d < 3:
                        dve.wait_ge(part_done, 12 * g + 3 * v + d + 1)
                    else:
                        dve.wait_ge(unit_done, U_PEER + 8 * g + EG + v + 1)
                    dve.tensor_tensor(two(Rt[:, dt, :]), two(Rt[:, dt, :]), acc(dt % 2), ALU.add).then_inc(out_evac, 1)

            dve.wait_ge(out_evac, 1 + KT_N * GROUPS)
            for part in (mv_hi, mv_lo):
                for k in range(KT_N):
                    last = dve.scalar_tensor_tensor(Rt[:, k, :], part[:, k, :].bitcast(f32), ALPHA, Rt[:, k, :],
                                                    ALU.mult, ALU.add)
                    if part is mv_lo:
                        last.then_inc(res_done, 1)
                if part is mv_hi:
                    own.done(last)
                    own.wait()
            dve.wait_ge(res_done, KT_N)
            layer_norm(1)


def kernel(**inputs):
    import concourse.bacc as _bacc
    from concourse import mybir as _mybir
    from concourse.bass_utils import run_bass_kernel_spmd as _run

    a = {k: np.asarray(v) for k, v in inputs.items()}
    f = np.float32
    x = np.concatenate([a["x_prompt"].reshape(SEQ, D), a["x_sample"].reshape(-1, D)], 0)
    x_t = np.ascontiguousarray(x.T).reshape(KT_N, P, T)

    order = np.array([h for j in range(PAIRS) for h in (j, PAIRS + j)])

    def units(w):
        rows, cols = w.shape
        return w.reshape(rows // P, P, cols // P, P).transpose(2, 1, 0, 3).reshape(cols // P, P, rows)

    w_in = a["w_in"]
    cut = np.cumsum([0, 1024, 1024, 1024, 1024, 128, 128, 2048, 2048])
    qa, ka, va, qb, kb, vb, ga, gb = (w_in[:, cut[i]:cut[i + 1]] for i in range(8))
    qb = qb.reshape(D, 16, HD)[:, order].reshape(D, 1024)
    wpb = a["w_proj_b"].reshape(16, HD, D)[order].reshape(1024, D)
    ws = np.empty((UNITS, P, D), f)
    ws[U_QKV:U_GATE] = np.concatenate([units(w) for w in (ka, va, kb, vb, qa, qb)], 0)
    ws[U_GATE:U_PROJ:2] = units(ga)
    ws[U_GATE + 1:U_PROJ:2] = units(gb)
    ws[U_PROJ:U_OUT] = units(np.concatenate([a["w_proj_a"], wpb], 0))
    ws[U_OUT:U_QUERY] = units(a["w_out"])
    ws[U_QUERY:U_PEER] = units(a["peer_w_query"])
    peer = ws[U_PEER:].reshape(GROUPS, 2, EG, P, D)
    peer[:, 0] = a["peer_u"].reshape(GROUPS, EG, KEYS, KT_N, P).transpose(0, 1, 4, 3, 2).reshape(GROUPS, EG, P, D)
    peer[:, 1] = a["peer_v"].reshape(GROUPS, EG, KEYS, 4, 4, P).transpose(0, 3, 2, 4, 1, 5).reshape(GROUPS, 4, P, D)

    cka = a["cache_a_k"].reshape(DEC_B, PAST, PAIRS, 2 * HD).transpose(2, 3, 0, 1).reshape(PAIRS, P, DEC_B * PAST)
    cva = a["cache_a_v"].reshape(DEC_B, PAST, PAIRS, 2 * HD).transpose(2, 1, 0, 3).reshape(PAIRS, P, DEC_B * P)
    ckb = a["cache_b_k"].reshape(DEC_B, PAST, 2 * HD).transpose(2, 0, 1).reshape(P, DEC_B * PAST)
    cvb = a["cache_b_v"].reshape(DEC_B, PAST, 2 * HD).transpose(1, 0, 2).reshape(P, DEC_B * P)

    rext = np.pad(a["rel_bias_table"], ((0, 0), (0, 383)), mode="edge")[:, ::-1]
    negs = np.full((16, 64, 64), NEG, f)
    slope = np.exp2(-8.0 * np.arange(1, 17) / 16).astype(f)[order]
    q, c = np.arange(P)[:, None], np.arange(256)[None]
    seen = (q + P) // 64 - c // 64
    bp_b = np.where((seen >= 0) & (seen <= 2), -slope[:, None, None] * np.abs(q + P - c).astype(f), f(NEG)).astype(f)
    bs_b = (-slope[:, None, None] * np.abs(q % DEC_T + PAST - np.arange(144)[None]).astype(f)).astype(f)
    bmask = np.where(q // DEC_T == np.arange(P)[None] // DEC_T, f(0), f(NEG))
    consts = np.concatenate([np.eye(P), np.ones((P, P)), np.tile(np.arange(P), (P, 1)), bmask], 1).astype(f)
    sinks = np.tile(a["b_sinks"][order][None], (P, 1))
    lnp = np.concatenate([a[n].reshape(KT_N, P).T for n in ("ln1_g", "ln1_b", "ln2_g", "ln2_b")], 1)
    subk = np.concatenate([a["peer_sub_keys_1"].T, a["peer_sub_keys_2"].T], 1)

    nc = _bacc.Bacc("TRN2", target_bir_lowering=False, num_devices=1)
    arrays, args = {}, []
    for name, arr in (("x_t", x_t), ("wstream", ws), ("cka", cka), ("cva", cva), ("ckb", ckb), ("cvb", cvb),
                      ("rext", rext), ("negs", negs), ("bp_b", bp_b), ("bs_b", bs_b), ("sinks", sinks), ("lnp", lnp),
                      ("subk", subk), ("consts", consts)):
        arrays["in_" + name] = np.ascontiguousarray(arr)
        args.append(nc.dram_tensor("in_" + name, arr.shape, _mybir.dt.from_np(arr.dtype), kind="ExternalInput").ap())
    args.append(nc.dram_tensor("out_p", (N_QKV, P, T), _mybir.dt.float32, kind="ExternalOutput").ap())
    args.append(nc.dram_tensor("out_y", (KT_N, P, T), _mybir.dt.float32, kind="ExternalOutput").ap())
    build(nc, *args)
    r = _run(nc, [arrays], core_ids=[0]).results[0]
    p = np.asarray(r["out_p"])
    y = np.asarray(r["out_y"]).reshape(D, T).T

    def heads(lo, n):
        return np.ascontiguousarray(p[lo:lo + n].reshape(n * P, T).T).reshape(T, n * 2, HD)

    k_a, v_a, k_b, v_b = heads(0, 8), heads(8, 8), heads(16, 1), heads(17, 1)
    prompt = lambda t, n: np.ascontiguousarray(t[SEQ - n:SEQ])[None]
    sample = lambda t: np.ascontiguousarray(t[SEQ:]).reshape((DEC_B, DEC_T) + t.shape[1:])
    return (np.ascontiguousarray(y[:SEQ])[None], np.ascontiguousarray(y[SEQ:]).reshape(DEC_B, DEC_T, D),
            prompt(k_a, SEQ), prompt(v_a, SEQ), prompt(k_b, 128), prompt(v_b, 128),
            sample(k_a), sample(v_a), sample(k_b), sample(v_b))
```

```python
from contextlib import ExitStack

import numpy as np
import concourse.bass as bass
from concourse import mybir

P = 128
D = 2048
KT_N = D // P
SEQ, DEC_B, DEC_T = 512, 8, 16
T = SEQ + DEC_B * DEC_T
HALF = T // 2
NB = T // P
PAST = 128
HD = 64
PAIRS = 8
PH, TOPK, KEYS = 8, 16, 128
EPS = 1e-5
ALPHA = float(2.0 ** 0.25)
SCALE = HD ** -0.5
NEG = -1e30
EG = 4
GROUPS = KEYS // EG
GT = 32
GBLK = SEQ // GT
TAIL = 4
EARLY = 5
N_EARLY = EG * EARLY
PICKS = PH * TOPK
STEPS_G = 2 * PICKS // GROUPS

N_QKV, N_GATE, N_PROJ, N_OUT, N_QUERY = 34, 32, 16, 16, 16
U_QKV = 0
U_GATE = U_QKV + N_QKV
U_PROJ = U_GATE + N_GATE
U_OUT = U_PROJ + N_PROJ
U_QUERY = U_OUT + N_OUT
U_PEER = U_QUERY + N_QUERY
UNITS = U_PEER + 2 * EG * GROUPS
ROW_KB, ROW_QA, ROW_QB = 16, 18, 26


class Own:

    def __init__(self, eng, sem, apart):
        self.eng, self.sem, self.apart, self.n, self.off = eng, sem, apart, 0, 0

    def done(self, ins):
        ins.then_inc(self.sem, 1)
        self.n += 1

    def wait(self):
        self.eng.wait_ge(self.sem, self.off + self.n)

    def wait_apart(self):
        self.wait()
        self.eng.sem_inc(self.apart, 1)

    def enter(self, i, per):
        self.start, self.per = self.n, per
        self.off = i * per

    def leave(self, trips):
        assert self.n - self.start == self.per, (self.n - self.start, self.per)
        self.n, self.off = self.start + self.per * trips, 0


def build(nc, x_t, wstream, u_rows, v_rows, cka, cva, ckb, cvb, rext, negs, bp_b, bs_b, sinks, lnp, subk, consts, pt_out, y_out):
    f32, f32r, u32 = mybir.dt.float32, mybir.dt.float32r, mybir.dt.uint32
    ALU, ACT = mybir.AluOpType, mybir.ActivationFunctionType
    AX = mybir.AxisListType
    ds = bass.ds

    with ExitStack() as ctx:
        def dram(name, shape):
            return nc.dram_tensor(name, shape, f32).ap()

        def sb(name, shape, dt=f32):
            return ctx.enter_context(nc.sbuf_tensor(name, shape, dt))

        def sem(name):
            return ctx.enter_context(nc.semaphore(name))

        g_s = dram("gate_scratch", (N_GATE, P, T))
        y_s = dram("attn_scratch", (KT_N, P, T))
        m_s = dram("merge_scratch", (KT_N, P, T))
        bp_a = dram("bias_prompt_a", (16, P, 512))
        bs_a = dram("bias_sample_a", (16, P, 144))
        a_s = dram("early_act", (N_EARLY, P, SEQ))
        G_s = dram("gate_matrix", (GBLK, P, KEYS, GT))

        raw = [sb(f"w_raw{s}", [P, D]) for s in range(2)]
        w_hi = [sb(f"w_hi{s}", [P, D], f32r) for s in range(2)]
        w_lo = [sb(f"w_lo{s}", [P, D], f32r) for s in range(2)]
        mv_hi = sb("mv_hi", [P, KT_N, T], f32r)
        mv_lo = sb("mv_lo", [P, KT_N, T], f32r)
        R = sb("work", [P, KT_N * T])
        ww_hi = sb("ww_hi", [P, EG, SEQ], f32r)
        ww_lo = sb("ww_lo", [P, EG, SEQ], f32r)
        W2 = sb("work2", [P, 5120])
        idx8 = sb("idx8", [P, STEPS_G], u32)
        cst = sb("cst", [P, 4 * P])
        subkt = sb("subkt", [P, 2 * KEYS])
        sinkt = sb("sinkt", [P, 16])
        lnt = sb("lnt", [P, 4 * KT_N])
        small = sb("small", [P, 16])

        ident, ones, iota, bmask = (cst[:, P * i:P * i + P] for i in range(4))
        Rt = R[:, :].rearrange("p (k t) -> p k t", k=KT_N)

        def area(at, n):
            return R[:, at:at + n]
        ck_t, cv_t = area(0, 1024), area(1024, 1024)
        bp_t = area(2048, 1024).rearrange("p (h c) -> p h c", h=2)
        bs_t = area(3072, 288).rearrange("p (h c) -> p h c", h=2)
        q_t, k_t, v_t = area(3360, T), area(4000, T), area(4640, T)
        vn = area(5280, T)
        s_sb = [area(5920, 512), area(6432, 512)]
        pt_sb = [area(6944, 512), area(7456, 512)]
        st_sb = [area(7968, P), area(8096, P)]
        y_t = area(8224, T)
        mx = [small[:, s:s + 1] for s in range(2)]
        nmax = [small[:, 2 + s:3 + s] for s in range(2)]
        rsum = [small[:, 4 + s:5 + s] for s in range(2)]
        esink = [small[:, 6 + s:7 + s] for s in range(2)]
        rden = [small[:, 8 + s:9 + s] for s in range(2)]
        den = [small[:, 10 + s:11 + s] for s in range(2)]

        ev = [W2[:, T * s:T * s + T] for s in range(2)]
        gate_t = [W2[:, 2 * T * (s + 1):2 * T * (s + 2)] for s in range(2)]
        x_res = [W2[:, 2 * T + T * s:3 * T + T * s] for s in range(2)]
        mean_t, rstd_t = W2[:, 0:T], W2[:, T:2 * T]
        sq_t = x_res
        act_t = [W2[:, SEQ * s:SEQ * s + SEQ] for s in range(2)]
        pick_t = [W2[:, SEQ * (q + 2):SEQ * (q + 3)] for q in range(3)]
        oh1 = W2[:, 5 * SEQ:5 * SEQ + 8 * P].rearrange("p (n e) -> p n e", n=8)
        oh2 = ww_hi[:, :, :].rearrange("p e t -> p (e t)")[:, 0:8 * P].rearrange("p (n e) -> p n e", n=8)
        G4 = W2[:, 2 * SEQ:6 * SEQ].rearrange("p (b e t) -> p b e t", b=GBLK, e=EG)
        r_acc = R[:, 0:KT_N * SEQ].rearrange("p (k t) -> p k t", k=KT_N)
        r_smp = R[:, KT_N * SEQ:KT_N * T].rearrange("p (k t) -> p k t", k=KT_N)
        rows_t = [W2[:, 6 * SEQ:10 * SEQ], R[:, KT_N * SEQ:KT_N * T]]
        gate_n, idx_n, act_n = cst[:, 3 * P:4 * P], subkt[:, 0:P].bitcast(u32), subkt[:, P:2 * P]
        dots = sb("dots", [P, STEPS_G])

        qe = [area(0, T), area(T, T)]
        sc_sb = [area(1280, T), area(1920, T)]
        sc2 = area(2560, T)
        cand, cand2 = area(3200, 1280), area(4480, 1280)
        val = area(5760, 160).rearrange("p (b s k) -> p b s k", b=NB, s=2)
        idx_f = area(5920, 160).rearrange("p (b s k) -> p b s k", b=NB, s=2)
        pick_g = area(6080, T).rearrange("p (b k) -> p b k", b=NB)
        c_f = [area(6720, 80), area(6800, 80)]
        eq = area(6880, 1280)
        pick_e = [area(8160, T).rearrange("p (b k) -> p b k", b=NB), area(8800, T).rearrange("p (b k) -> p b k", b=NB)]
        idx_u = area(9440, 160).bitcast(u32).rearrange("p (b s k) -> p b s k", b=NB, s=2)
        ci_u = area(9600, 80).bitcast(u32)
        cp_u = [area(9680, 80).bitcast(u32), area(9760, 80).bitcast(u32)]
        psum_g = area(9840, 40)
        top_v = area(9880, 80)
        g_buf = [area(w * GT * KEYS, GT * KEYS).rearrange("p (e t) -> p e t", t=GT) for w in range(2)]

        banks = ctx.enter_context(nc.psum_tensor("banks", [P, 8, 512], f32))

        def acc(s):
            return banks[:, 2 * s:2 * s + 2, 0:HALF]

        nat = banks[:, 4:8, :].rearrange("p b c -> p (b c)")

        def two(ap):
            return ap.rearrange("p (a t) -> p a t", a=2)

        s_bank = [banks[:, 4, :], banks[:, 5, :]]
        t_bank, o_bank = banks[:, 6, :], banks[:, 7, :]

        ln_parts = [[(lambda k, h=h: Rt[:, k, HALF * h:HALF * h + HALF], slice(HALF * h, HALF * h + HALF),
                      lambda z, h=h: acc(z)[:, h, :]) for h in range(2)],
                    [(lambda k: r_acc[:, k, :], slice(0, SEQ), lambda z: banks[:, 2 * z, 0:SEQ]),
                     (lambda k: r_smp[:, k, :], slice(SEQ, T), lambda z: banks[:, 2 * z + 1, 0:T - SEQ])]]

        def sc_parts(s):
            return banks[:, 4 + 2 * s, :], banks[:, 5 + 2 * s, 0:P]

        raw_full = [sem(f"raw_full{s}") for s in range(2)]
        hi_done, split_done, unit_done = sem("hi_done"), sem("split_done"), sem("unit_done")
        mv_in = [sem(f"mv_in{q}") for q in range(4)]
        mvh_done, mv_ready = sem("mvh_done"), sem("mv_ready")
        const_in, tab_done = sem("const_in"), sem("tab_done")
        qkv_evac, gate_evac = sem("qkv_evac"), sem("gate_evac")
        qkv_stored = [sem(f"qkv_stored{s}") for s in range(2)]
        gate_stored = [sem(f"gate_stored{s}") for s in range(2)]
        att_in, s_full, s_taken, nmax_ready, e_ready, p_ready = (
            sem(n) for n in ("att_in", "s_full", "s_taken", "nmax_ready", "e_ready", "p_ready"))
        t_full, t_taken, o_full, o_taken, y_stored = (
            sem(n) for n in ("t_full", "t_taken", "o_full", "o_taken", "y_stored"))
        gate_in = [sem(f"gate_in{s}") for s in range(2)]
        sig_done, za_done, z_taken, msum_done = (sem(n) for n in ("sig_done", "za_done", "z_taken", "msum_done"))
        m_stored = [sem(f"m_stored{s}") for s in range(2)]
        x_in = [sem(f"x_in{s}") for s in range(2)]
        r_done = sem("r_done")
        ln = [{n: sem(f"ln{p}_{n}") for n in ("sum", "centered", "squared", "sq_used", "var", "std", "scaled", "out")}
              for p in range(2)]
        y_out_done = sem("y_out_done")
        res_done = sem("res_done")
        q_evac, sc_full, sc_taken, topk_done = (sem(n) for n in ("q_evac", "sc_full", "sc_taken", "topk_done"))
        gexp_in, gexp_done, picks_done, picks_full, picks_taken = (
            sem(n) for n in ("gexp_in", "gexp_done", "picks_done", "picks_full", "picks_taken"))
        oh_ready, g_full, g_evac = sem("oh_ready"), sem("g_full"), sem("g_evac")
        act_stored = [sem(f"act_stored{s}") for s in range(2)]
        act_in = [sem(f"act_in{s}") for s in range(2)]
        rows_in = [sem(f"rows_in{s}") for s in range(2)]
        idx_ready, idx8_ready, rows_used, nat_ready, act_n_ready, act_n_gelu, nat_out, nat_t, smp_ready = (
            sem(n) for n in ("idx_ready", "idx8_ready", "rows_used", "nat_ready", "act_n_ready", "act_n_gelu",
                             "nat_out", "nat_t", "smp_ready"))
        g_stored = [sem(f"g_stored{w}") for w in range(2)]
        g4_in, gelu_done, w_prod, wwh_done, w_ready, part_done, out_evac = (
            sem(n) for n in ("g4_in", "gelu_done", "w_prod", "wwh_done", "w_ready", "part_done", "out_evac"))
        dve_own = sem("dve_own")
        dve_apart, pool_apart = sem("dve_apart"), sem("pool_apart")

        STEPS = [(hh, i) for hh in range(2) for i in range(4)] + [(0, "sample"), (1, "sample")]
        NS = len(STEPS)

        def width(mix, i):
            if i == "sample":
                return 2 * P
            return P * (i + 1) if mix == "a" else P * min(i + 1, 2)

        T_USES = {m: ([("v", 0), ("v", 1)] if m == "a" else [])
                  + [("t", t) for t in range(6)] + [("c", 0), ("t", 6), ("c", 1)] + [("t", t) for t in range(7, NS)]
                  for m in "ab"}
        T_BASE = {"a": 0, "b": len(T_USES["a"]) * PAIRS + 2}
        STEP_BASE = {"a": 0, "b": NS * PAIRS}
        IN_BASE = {"a": 0, "b": 16 * (7 * PAIRS + 4)}
        IN_PER = {"a": 16 * 7, "b": 16 * 3}

        def t_use(mix, j, what, extra=0):
            return T_BASE[mix] + j * len(T_USES[mix]) + T_USES[mix].index(what) + extra

        block = ctx.enter_context(nc.Block())

        @block.sync
        def _(sp):
            for s in range(2):
                sp.dma_start(raw[s][:, :], wstream[s]).then_inc(raw_full[s], 16)
            with sp.Fori(1, UNITS // 2) as i:
                for s in range(2):
                    sp.wait_ge(split_done, 2 * i + s - 1)
                    sp.dma_start(raw[s][:, :], wstream[ds(2 * i + s, 1)].rearrange("a p c -> p (a c)")) \
                        .then_inc(raw_full[s], 16)

        @block.gpsimd
        def _(pool):
            def split(s, pair):
                pool.wait_ge(raw_full[s], 16 * pair + 16)
                pool.sem_inc(pool_apart, 1)
                pool.tensor_scalar(w_hi[s][:, :], raw[s][:, :], 1.0, 0.0, ALU.mult, ALU.add).then_inc(hi_done, 1)
                pool.wait_ge(hi_done, 2 * pair + s + 1)
                pool.tensor_tensor(w_lo[s][:, :], raw[s][:, :], w_hi[s][:, :].bitcast(f32), ALU.subtract) \
                    .then_inc(split_done, 1)

            def split_next(s, pair):
                pool.wait_ge(unit_done, 2 * pair + s - 1)
                split(s, pair)

            for s in range(2):
                split(s, 0)
            with pool.Fori(1, (U_PEER + N_EARLY) // 2) as i:
                for s in range(2):
                    split_next(s, i)

            def gather(table, g, c):
                if c == 0:
                    pool.wait_ge(idx8_ready, g + 1)
                pool.wait_ge(rows_used, STEPS_G * g + c + 1)
                pool.sem_inc(pool_apart, 1)
                pool.indirect_dma_start(rows_t[c % 2], None, table,
                                        bass.IndirectOffsetOnAxis(ap=idx8[:, c:c + 1], axis=0)) \
                    .then_inc(rows_in[c % 2], 16)

            def group_indices(g, first):
                for s in range(2):
                    pool.wait_ge(rows_in[s], 16 * (STEPS_G // 2) * g)
                pool.sem_inc(pool_apart, 1)
                pool.tensor_copy(idx8[:, :], idx_n[:, ds(STEPS_G * (g - first), STEPS_G)]).then_inc(idx8_ready, 1)

            pool.wait_ge(idx_ready, 1)
            with pool.Fori(0, EARLY) as g:
                group_indices(g, 0)
                for v in range(EG):
                    split_next(v % 2, (U_PEER + N_EARLY) // 2 + 2 * g + v // 2)
                    gather(u_rows, g, 2 * v)
                    gather(u_rows, g, 2 * v + 1)
            for table, lo, hi in ((u_rows, EARLY, GROUPS // 2), (v_rows, GROUPS // 2, GROUPS)):
                with pool.Fori(lo, hi) as g:
                    group_indices(g, 0 if table is u_rows else GROUPS // 2)
                    for n in range(2 * EG):
                        split_next(n % 2, U_PEER // 2 + EG * g + n // 2)
                        gather(table, g, n)

        @block.tensor
        def _(pe):
            def k_step(s, k, dst, k_first, k_last, phase):
                if phase is not None and k % 4 == 0:
                    pe.wait_ge(mv_ready, KT_N * phase + k + 4)
                for n, (a, b) in enumerate(((w_hi, mv_hi), (w_hi, mv_lo), (w_lo, mv_hi))):
                    for h in range(2):
                        last = pe.matmul(acc(dst)[:, h, :], a[s][:, P * k:P * k + P], b[:, k, HALF * h:HALF * h + HALF],
                                         start=(k == k_first and n == 0), stop=(k == k_last and n == 2))
                return last

            def unit(s, n, free, phase):
                pe.wait_ge(split_done, n + 1)
                pe.wait_ge(*free)
                for k in range(KT_N):
                    last = k_step(s, k, s, 0, KT_N - 1, phase)
                last.then_inc(unit_done, 1)

            with pe.Fori(0, N_QKV // 2) as i:
                for s in range(2):
                    unit(s, U_QKV + 2 * i + s, (qkv_evac, 2 * i + s + 1), 0)

            def scores(mix, j, t):
                hh, i = STEPS[t]
                rows = slice(HD * hh, HD * hh + HD)
                bank = s_bank[t % 2]
                if t >= 1:
                    pe.wait_ge(s_taken, STEP_BASE[mix] + NS * j + t - 1)
                if i == "sample":
                    pe.wait_ge(t_taken, t_use(mix, j, ("c", hh), 1))
                    pe.transpose(bank[:, 0:P], st_sb[hh][:, :], ident)
                    last = pe.matmul(bank[:, P:2 * P], q_t[rows, SEQ:T], k_t[rows, SEQ:T], start=True, stop=True)
                else:
                    w = width(mix, i)
                    end = P * (i + 1)
                    last = pe.matmul(bank[:, 0:w], q_t[rows, P * i:end], k_t[rows, end - w:end], start=True, stop=True)
                last.then_inc(s_full, 1)

            def transpose_p(mix, j, t):
                w = width(mix, STEPS[t][1])
                pe.wait_ge(p_ready, STEP_BASE[mix] + NS * j + t + 1)
                pe.wait_ge(t_taken, t_use(mix, j, ("t", t)))
                for c in range(w // P):
                    last = pe.transpose(t_bank[:, P * c:P * c + P], s_sb[t % 2][:, P * c:P * c + P], ident)
                last.then_inc(t_full, 1)

            def cached_scores(mix, j, hh):
                rows = slice(HD * hh, HD * hh + HD)
                pe.wait_ge(t_taken, t_use(mix, j, ("c", hh)))
                for b in range(DEC_B):
                    c = DEC_T * b
                    last = pe.matmul(t_bank[:, c:c + DEC_T], ck_t[rows, P * b:P * b + P],
                                     q_t[rows, SEQ + c:SEQ + c + DEC_T], start=True, stop=True)
                last.then_inc(t_full, 1)

            def values(mix, j, t):
                hh, i = STEPS[t]
                rows, pt = slice(HD * hh, HD * hh + HD), pt_sb[t % 2]
                pe.wait_ge(t_taken, t_use(mix, j, ("t", t), 1))
                pe.wait_ge(o_taken, STEP_BASE[mix] + NS * j + t)
                o = o_bank[rows, 0:P]
                if i == "sample":
                    for b in range(DEC_B):
                        c = DEC_T * b
                        pe.matmul(o[:, c:c + DEC_T], cv_t[:, P * b + HD * hh:P * b + HD * hh + HD],
                                  pt[:, c:c + DEC_T], start=(b == 0), stop=False)
                    last = pe.matmul(o, vn[:, P * 4 + HD * hh:P * 4 + HD * hh + HD], pt[:, P:2 * P],
                                     start=False, stop=True)
                else:
                    nk = width(mix, i) // P
                    for c in range(nk):
                        kb = i + 1 - nk + c
                        last = pe.matmul(o, vn[:, P * kb + HD * hh:P * kb + HD * hh + HD], pt[:, P * c:P * c + P],
                                         start=(c == 0), stop=(c == nk - 1))
                last.then_inc(o_full, 1)

            def transpose_v(first, use):
                pe.wait_ge(t_taken, use)
                for b in (range(4) if first else (4,)):
                    last = pe.transpose(t_bank[:, P * (b % 4):P * (b % 4) + P], v_t[:, P * b:P * b + P], ident)
                last.then_inc(t_full, 1)

            def attention_pair(mix, j):
                first = U_GATE + 2 * (j + (PAIRS if mix == "b" else 0))
                k_steps = [(s, k) for s in range(2) for k in range(KT_N)]

                def gemm(n):
                    for _ in range(n):
                        s, k = k_steps.pop(0)
                        if k == 0:
                            pe.wait_ge(split_done, first + s + 1)
                            pe.wait_ge(gate_evac, first - U_GATE + s + 1)
                        last = k_step(s, k, s, 0, KT_N - 1, None)
                        if k == KT_N - 1:
                            last.then_inc(unit_done, 1)

                gemm(10)
                pe.wait_ge(att_in, IN_BASE[mix] + IN_PER[mix] * j + IN_PER[mix])
                if mix == "a":
                    transpose_v(True, t_use(mix, j, ("v", 0)))
                gemm(2)
                if mix == "a":
                    transpose_v(False, t_use(mix, j, ("v", 1)))
                for t in range(NS + 2):
                    if t < NS:
                        scores(mix, j, t)
                    if k_steps:
                        gemm(2)
                    if 1 <= t <= NS:
                        transpose_p(mix, j, t - 1)
                    if t >= 2:
                        values(mix, j, t - 2)
                    if t in (6, 7):
                        cached_scores(mix, j, t - 6)
                assert not k_steps

            pe.wait_ge(const_in, 64)
            with pe.Fori(0, PAIRS) as j:
                attention_pair("a", j)
            pe.wait_ge(att_in, IN_BASE["b"])
            transpose_v(True, T_BASE["b"] - 2)
            transpose_v(False, T_BASE["b"] - 1)
            with pe.Fori(0, PAIRS) as j:
                attention_pair("b", j)

            with pe.Fori(0, N_PROJ // 2) as i:
                for s in range(2):
                    m = 2 * i + s
                    pe.wait_ge(split_done, U_PROJ + m + 1)
                    for z in range(2):
                        pe.wait_ge(z_taken, 2 * m + z + 1)
                        for k in range(8 * z, 8 * z + 8):
                            last = k_step(s, k, z, 8 * z, 8 * z + 7, 1)
                        last.then_inc((za_done, unit_done)[z], 1)

            with pe.Fori(0, N_OUT // 2) as i:
                for s in range(2):
                    unit(s, U_OUT + 2 * i + s, (r_done, 2 * i + s + 1), 2)

            def layer_norm(q, ready, total):
                for k in range(KT_N):
                    pe.wait_ge(ready, total(k))
                    for (src, cols, out) in ln_parts[q]:
                        last = pe.matmul(out(0), ones, src(k), start=(k == 0), stop=(k == KT_N - 1))
                last.then_inc(ln[q]["sum"], 1)
                for k in range(KT_N):
                    pe.wait_ge(ln[q]["squared"], k + 1)
                    for (src, cols, out) in ln_parts[q]:
                        last = pe.matmul(out(1), ones, sq_t[k % 2][:, cols], start=(k == 0), stop=(k == KT_N - 1))
                    last.then_inc(ln[q]["sq_used"], 1)

            layer_norm(0, r_done, lambda k: max(k + 3, N_OUT + 1))

            def key_scores(s, c):
                pe.wait_ge(q_evac, c + 3)
                pe.wait_ge(sc_taken, c + 1)
                four, one = sc_parts(s)
                for b in range(NB):
                    out = four[:, P * b:P * b + P] if b < 4 else one
                    last = pe.matmul(out, qe[s][:, P * b:P * b + P], subkt[:, KEYS * s:KEYS * s + KEYS],
                                     start=True, stop=True)
                last.then_inc(sc_full, 1)

            with pe.Fori(0, N_QUERY // 2) as i:
                unit(0, U_QUERY + 2 * i, (q_evac, 2 * i + 1), 3)
                pe.wait_ge(split_done, U_QUERY + 2 * i + 2)
                pe.wait_ge(q_evac, 2 * i + 2)
                for k in range(KT_N):
                    last = k_step(1, k, 1, 0, KT_N - 1, 3)
                    if k == 3:
                        key_scores(0, 2 * i)
                last.then_inc(unit_done, 1)
                key_scores(1, 2 * i + 1)

            def act_step(s, k, bank):
                for n, (a, b) in enumerate(((w_hi, mv_hi), (w_hi, mv_lo), (w_lo, mv_hi))):
                    last = pe.matmul(banks[:, bank, :], a[s][:, P * k:P * k + P], b[:, k, 0:SEQ],
                                     start=(k == 0 and n == 0), stop=(k == KT_N - 1 and n == 2))
                if k == KT_N - 1:
                    last.then_inc(unit_done, 1)

            pe.wait_ge(sc_taken, 2 + N_QUERY)
            pe.wait_ge(q_evac, 2 + N_QUERY)
            for n in range(TAIL):
                pe.wait_ge(split_done, U_PEER + n + 1)
                if n >= 2:
                    pe.wait_ge(gelu_done, n - 1)
                for k in range(KT_N):
                    act_step(n % 2, k, n % 2)

            pe.wait_ge(picks_done, 1)
            for q, src in enumerate((pick_g, pick_e[0], pick_e[1])):
                for b in range(SEQ // P):
                    last = pe.transpose(banks[:, 4 + q, P * b:P * b + P], src[:, b, :], ident)
                last.then_inc(picks_full, 1)
            pe.wait_ge(picks_taken, 3)
            for k in range(KT_N):
                for n, part in enumerate((mv_hi, mv_lo)):
                    last = pe.matmul(nat[:, P * k:P * k + P], part[:, k, SEQ:T].bitcast(f32), ident,
                                     start=(n == 0), stop=(n == 1))
            last.then_inc(nat_ready, 1)

            pe.sem_inc(g_full, 2)
            with pe.Fori(0, GBLK // 2) as i:
                for q in range(2 * GT // 4):
                    for k in (2 * q, 2 * q + 1):
                        s, n = k // KT_N, TAIL + 2 * i + k // KT_N
                        if k % KT_N == 0:
                            pe.wait_ge(split_done, U_PEER + n + 1)
                            pe.wait_ge(gelu_done, n - 1)
                        act_step(s, k % KT_N, s)
                    pe.wait_ge(oh_ready, 16 * i + q + 1)
                    pe.wait_ge(g_evac, 16 * i + q + 1)
                    for t in range(4):
                        n = 4 * (q % 2) + t
                        last = pe.matmul(banks[:, 2 + q % 2, P * t:P * t + P], oh2[:, n, :].bitcast(f32), oh1[:, n, :],
                                         start=True, stop=True)
                    last.then_inc(g_full, 1)
            pe.wait_ge(g_evac, 2 + SEQ // 4)
            pe.wait_ge(gelu_done, N_EARLY)

            def out_units(g, first, early):
                for v in range(EG):
                    s = v % 2
                    pe.wait_ge(split_done, first + v + 1)
                    for d in range(4):
                        dt = 4 * v + d
                        if dt < 4 and not early:
                            pe.wait_ge(gelu_done, 4 * g + dt + 1)
                        else:
                            pe.wait_ge(out_evac, 16 * g + dt + 1)
                        for e in range(EG):
                            if dt == 0:
                                pe.wait_ge(w_ready, 4 * g + e + 3)
                            for n, (a, b) in enumerate(((w_hi, ww_hi), (w_hi, ww_lo), (w_lo, ww_hi))):
                                at = P * (EG * d + e)
                                last = pe.matmul(banks[:, dt % 4, :], a[s][:, at:at + P], b[:, e, :],
                                                 start=(e == 0 and n == 0), stop=(e == EG - 1 and n == 2))
                        last.then_inc(unit_done if d == 3 else part_done, 1)

            with pe.Fori(0, EARLY) as g:
                out_units(g, U_PEER + N_EARLY + EG * g, True)
            with pe.Fori(EARLY, GROUPS) as g:
                for e in range(EG):
                    pe.wait_ge(split_done, U_PEER + 8 * g + e + 1)
                    pe.wait_ge(out_evac, 16 * g + e + 1)
                    for k in range(KT_N):
                        act_step(e % 2, k, e)
                out_units(g, U_PEER + 8 * g + EG, False)

            pe.wait_ge(out_evac, 4 + KT_N * GROUPS)
            pe.wait_ge(nat_out, 1)
            for k in range(KT_N):
                last = pe.transpose(banks[:, k // 4, P * (k % 4):P * (k % 4) + P], rows_t[0][:, P * k:P * k + P], ident)
            last.then_inc(nat_t, 1)
            pe.wait_ge(smp_ready, 1)

            layer_norm(1, res_done, lambda k: k + 1)

        @block.scalar
        def _(act):
            act.dma_start(cst[:, :], consts).then_inc(const_in, 16)
            act.dma_start(subkt[:, :], subk).then_inc(const_in, 16)
            act.dma_start(sinkt[:, :], sinks).then_inc(const_in, 16)
            act.dma_start(lnt[:, :], lnp).then_inc(const_in, 16)

            def load_moving(src, phase, after):
                for w in after:
                    act.wait_ge(*w)
                for q in range(4):
                    act.dma_start(Rt[:, 4 * q:4 * q + 4, :], src[4 * q:4 * q + 4].rearrange("k p t -> p k t")) \
                        .then_inc(mv_in[q], 16)
                for k in range(KT_N):
                    if k % 4 == 0:
                        act.wait_ge(mv_in[k // 4], 16 * phase + 16)
                    act.activation(mv_hi[:, k, :], Rt[:, k, :], ACT.Copy).then_inc(mvh_done, 1)

            load_moving(x_t, 0, ())

            rt = rext.tensor
            n_r = rext.shape[1]
            act.dma_start(bp_a[:, 64:P, :], bass.AP(rt, 63, [[n_r, 16], [-1, 64], [1, 512]])).then_inc(tab_done, 16)
            act.dma_start(bp_a[:, 0:64, 0:448], bass.AP(rt, 127, [[n_r, 16], [-1, 64], [1, 448]])).then_inc(tab_done, 16)
            act.dma_start(bp_a[:, 0:64, 448:512], negs).then_inc(tab_done, 16)
            for b in range(DEC_B):
                act.dma_start(bs_a[:, DEC_T * b:DEC_T * b + DEC_T, :], bass.AP(rt, 383, [[n_r, 16], [-1, 16], [1, 144]])) \
                    .then_inc(tab_done, 16)

            act.sem_inc(qkv_evac, 2)
            with act.Fori(0, N_QKV // 2) as i:
                for s in range(2):
                    act.wait_ge(unit_done, 2 * i + s + 1)
                    act.wait_ge(qkv_stored[s], 16 * i)
                    act.activation(two(ev[s]), acc(s), ACT.Copy).then_inc(qkv_evac, 1)
                    act.wait_ge(qkv_evac, 2 * i + s + 3)
                    act.dma_start(pt_out[ds(2 * i + s, 1)].rearrange("a p t -> p (a t)"), ev[s]) \
                        .then_inc(qkv_stored[s], 16)

            def gate_evacuate(n, s, trip):
                act.wait_ge(unit_done, U_GATE + n + 1)
                act.wait_ge(gate_stored[s], 16 * trip)
                act.activation(two(ev[s]), acc(s), ACT.Copy).then_inc(gate_evac, 1)
                act.wait_ge(gate_evac, n + 3)
                act.dma_start(g_s[ds(n, 1)].rearrange("a p t -> p (a t)"), ev[s]).then_inc(gate_stored[s], 16)

            def take(mix, j, what):
                kind, t = what
                if kind == "v":
                    src, dst = (t_bank[:, 0:512], vn[:, 0:512]) if t == 0 else (t_bank[:, 0:P], vn[:, 512:T])
                elif kind == "c":
                    src, dst = t_bank[:, 0:P], st_sb[t][:, :]
                else:
                    w = width(mix, STEPS[t][1])
                    src, dst = t_bank[:, 0:w], pt_sb[t % 2][:, 0:w]
                    if t >= 2:
                        act.wait_ge(o_full, STEP_BASE[mix] + NS * j + t - 1)
                act.wait_ge(t_full, t_use(mix, j, what, 1))
                act.activation(dst, src, ACT.Copy).then_inc(t_taken, 1)

            def attention_pair(mix, j, pair):
                def load(dst, src):
                    act.dma_start(dst, src).then_inc(att_in, 16)

                def row(src, r):
                    return src[ds(r, 1)].rearrange("a p t -> p (a t)")

                if mix == "a":
                    load(q_t, row(pt_out, ROW_QA + j))
                    load(k_t, row(pt_out, j))
                    load(v_t, row(pt_out, 8 + j))
                    load(ck_t, row(cka, j))
                    load(cv_t, row(cva, j))
                    load(bp_t, bp_a[ds(2 * j, 2)].rearrange("h p c -> p h c"))
                    load(bs_t, bs_a[ds(2 * j, 2)].rearrange("h p c -> p h c"))
                else:
                    load(q_t, row(pt_out, ROW_QB + j))
                    load(bp_t[:, :, 256:512], bp_b[ds(2 * j, 2)].rearrange("h p c -> p h c"))
                    load(bs_t, bs_b[ds(2 * j, 2)].rearrange("h p c -> p h c"))
                if mix == "a":
                    take(mix, j, ("v", 0))
                    take(mix, j, ("v", 1))
                for t in range(NS + 1):
                    if t < NS:
                        w, step = width(mix, STEPS[t][1]), STEP_BASE[mix] + NS * j + t
                        act.wait_ge(nmax_ready, step + 1)
                        exp = act.activation(s_sb[t % 2][:, 0:w], s_sb[t % 2][:, 0:w], ACT.Exp, bias=nmax[t % 2],
                                             accum_out=rsum[t % 2])
                        if mix == "b":
                            col = 2 * j + STEPS[t][0]
                            exp = act.activation(esink[t % 2], sinkt[:, ds(col, 1)], ACT.Exp, bias=nmax[t % 2])
                        exp.then_inc(e_ready, 1)
                    if t >= 1:
                        take(mix, j, ("t", t - 1))
                    if t in (6, 7):
                        take(mix, j, ("c", t - 6))
                    if t == 4:
                        gate_evacuate(2 * pair, 0, pair)
                act.wait_ge(o_taken, STEP_BASE[mix] + NS * j + NS)
                act.dma_start(y_s[ds(pair, 1)].rearrange("a p t -> p (a t)"), y_t).then_inc(y_stored, 16)
                gate_evacuate(2 * pair + 1, 1, pair)

            act.sem_inc(gate_evac, 2)
            for s in range(2):
                act.wait_ge(qkv_stored[s], 16 * (N_QKV // 2))
            act.wait_ge(tab_done, 16 * (3 + DEC_B))
            act.wait_ge(mv_ready, KT_N)
            with act.Fori(0, PAIRS) as j:
                attention_pair("a", j, j)
            for dst, src in ((k_t, pt_out[ROW_KB]), (v_t, pt_out[ROW_KB + 1]), (ck_t, ckb), (cv_t, cvb)):
                act.dma_start(dst, src).then_inc(att_in, 16)
            for n in range(2):
                act.wait_ge(t_full, T_BASE["b"] - 1 + n)
                src, dst = (t_bank[:, 0:512], vn[:, 0:512]) if n == 0 else (t_bank[:, 0:P], vn[:, 512:T])
                act.activation(dst, src, ACT.Copy).then_inc(t_taken, 1)
            with act.Fori(0, PAIRS) as j:
                attention_pair("b", j, PAIRS + j)

            load_moving(y_s, 1, ((y_stored, 16 * 2 * PAIRS), (unit_done, U_PROJ)))
            for s in range(2):
                act.wait_ge(gate_stored[s], 16 * 2 * PAIRS)
            with act.Fori(0, N_PROJ // 2) as i:
                for s in range(2):
                    m = 2 * i + s
                    act.wait_ge(msum_done, m + 1)
                    act.dma_start(gate_t[s].rearrange("p (a t) -> p a t", a=2),
                                  g_s[ds(2 * m, 2)].rearrange("a p t -> p a t")).then_inc(gate_in[s], 16)
                    act.wait_ge(gate_in[s], 16 * i + 16)
                    act.activation(gate_t[s], gate_t[s], ACT.Sigmoid).then_inc(sig_done, 1)
                    act.wait_ge(msum_done, m + 3)
                    act.dma_start(m_s[ds(m, 1)].rearrange("a p t -> p (a t)"), ev[s]).then_inc(m_stored[s], 16)

            load_moving(m_s, 2, ((m_stored[0], 16 * (N_PROJ // 2)), (m_stored[1], 16 * (N_PROJ // 2)), (unit_done, U_OUT)))
            with act.Fori(0, N_OUT // 2) as i:
                for s in range(2):
                    act.wait_ge(r_done, 2 * i + s + 1)
                    act.dma_start(x_res[s], x_t[ds(2 * i + s, 1)].rearrange("a p t -> p (a t)")).then_inc(x_in[s], 16)

            def layer_norm(q, finish):
                for k in range(KT_N):
                    act.wait_ge(ln[q]["centered"], k + 1)
                    if k >= 2:
                        act.wait_ge(ln[q]["sq_used"], k - 1)
                    for (src, cols, out) in ln_parts[q]:
                        last = act.activation(sq_t[k % 2][:, cols], src(k), ACT.Square)
                    last.then_inc(ln[q]["squared"], 1)
                act.wait_ge(ln[q]["var"], 1)
                act.activation(rstd_t, rstd_t, ACT.Sqrt).then_inc(ln[q]["std"], 1)
                gain, shift = 2 * KT_N * q, 2 * KT_N * q + KT_N
                for k in range(KT_N):
                    act.wait_ge(ln[q]["scaled"], k + 1)
                    for (src, cols, out) in ln_parts[q]:
                        last = act.activation(src(k), src(k), ACT.Identity, bias=lnt[:, shift + k:shift + k + 1],
                                              scale=lnt[:, gain + k:gain + k + 1])
                    last.then_inc(ln[q]["out"], 1)
                    act.wait_ge(ln[q]["out"], k + 1)
                    finish(k)

            act.wait_ge(const_in, 64)
            layer_norm(0, lambda k: act.activation(mv_hi[:, k, :], Rt[:, k, :], ACT.Copy).then_inc(mvh_done, 1))

            act.wait_ge(mv_ready, 4 * KT_N)
            act.sem_inc(q_evac, 2)
            act.sem_inc(sc_taken, 2)
            with act.Fori(0, N_QUERY // 2) as i:
                for s in range(2):
                    c = 2 * i + s
                    act.wait_ge(unit_done, U_QUERY + c + 1)
                    act.activation(two(qe[s]), acc(s), ACT.Copy).then_inc(q_evac, 1)
                    act.wait_ge(sc_full, c + 1)
                    act.wait_ge(topk_done, c + 1)
                    four, one = sc_parts(s)
                    act.activation(sc_sb[s][:, 0:512], four, ACT.Copy)
                    act.activation(sc_sb[s][:, 512:T], one, ACT.Copy).then_inc(sc_taken, 1)

            def early_activation(n, s, trip):
                act.wait_ge(unit_done, U_PEER + n + 1)
                act.wait_ge(act_stored[s], 16 * trip)
                act.activation(act_t[s], banks[:, s, :], ACT.Gelu).then_inc(gelu_done, 1)
                act.wait_ge(gelu_done, n + 1)
                act.dma_start(a_s[ds(n, 1)].rearrange("a p t -> p (a t)"), act_t[s]).then_inc(act_stored[s], 16)

            for n in range(TAIL):
                early_activation(n, n % 2, n // 2)
            act.wait_ge(gexp_in, 1)
            flat = pick_g.rearrange("p b k -> p (b k)")
            act.activation(flat, flat, ACT.Exp).then_inc(gexp_done, 1)
            for q in range(3):
                act.wait_ge(picks_full, q + 1)
                act.activation(pick_t[q], banks[:, 4 + q, :], ACT.Copy).then_inc(picks_taken, 1)

            act.sem_inc(g_evac, 2)
            with act.Fori(0, GBLK // 2) as i:
                for q in range(2 * GT // 4):
                    w, qq = q // 8, q % 8
                    act.wait_ge(g_full, 16 * i + q + 3)
                    if qq == 0:
                        act.wait_ge(g_stored[w], 16 * i)
                    act.activation(g_buf[w][:, :, 4 * qq:4 * qq + 4],
                                   banks[:, 2 + q % 2, :].rearrange("p (t e) -> p e t", t=4), ACT.Copy).then_inc(g_evac, 1)
                    if qq == 7:
                        act.wait_ge(g_evac, 16 * i + q + 3)
                        act.dma_start(G_s[ds(2 * i + w, 1)].rearrange("a p e t -> p (a e t)"),
                                      g_buf[w].rearrange("p e t -> p (e t)")).then_inc(g_stored[w], 16)
                    if q in (8, 15):
                        early_activation(TAIL + 2 * i + q // 15, q // 15, TAIL // 2 + i)

            for w in range(2):
                act.wait_ge(g_stored[w], 16 * (GBLK // 2))
                act.wait_ge(act_stored[w], 16 * (N_EARLY // 2))

            def load_gates(g):
                act.wait_ge(w_prod, 4 * g)
                act.dma_start(G4.rearrange("p b e t -> p b (e t)"),
                              G_s[:, :, ds(EG * g, EG), :].rearrange("b p e t -> p b (e t)")).then_inc(g4_in, 16)

            def high_part(g, e):
                act.wait_ge(w_prod, 4 * g + e + 1)
                act.activation(ww_hi[:, e, :], act_t[e % 2], ACT.Copy).then_inc(wwh_done, 1)

            with act.Fori(0, EARLY) as g:
                load_gates(g)

                def load_act(e):
                    act.wait_ge(w_ready, 4 * g + e + 1)
                    act.dma_start(act_t[e % 2], a_s[ds(EG * g + e, 1)].rearrange("a p t -> p (a t)")) \
                        .then_inc(act_in[e % 2], 16)

                load_act(0)
                load_act(1)
                act.wait_ge(unit_done, U_PEER + N_EARLY + EG * g)
                for e in range(EG):
                    high_part(g, e)
                    if e < 2:
                        load_act(e + 2)

            def main_group(g):
                load_gates(g)
                for e in range(EG):
                    act.wait_ge(unit_done, U_PEER + 8 * g + e + 1)
                    act.wait_ge(w_ready, 4 * g + e + 1)
                    act.activation(act_t[e % 2], banks[:, e, :], ACT.Gelu).then_inc(gelu_done, 1)
                    high_part(g, e)

            with act.Fori(EARLY, GROUPS // 2) as g:
                main_group(g)
            act.wait_ge(act_n_ready, 1)
            act.activation(act_n, act_n, ACT.Gelu).then_inc(act_n_gelu, 1)
            with act.Fori(GROUPS // 2, GROUPS) as g:
                main_group(g)

            act.wait_ge(nat_t, 1)
            for n in range(4):
                last = act.activation(rows_t[1][:, SEQ * n:SEQ * n + SEQ], banks[:, n, :], ACT.Copy)
            last.then_inc(smp_ready, 1)

            def store_y(k):
                for (src, cols, out) in ln_parts[1]:
                    act.dma_start(y_out[k, :, cols], src(k)).then_inc(y_out_done, 16)

            layer_norm(1, store_y)
            act.wait_ge(y_out_done, 16 * 2 * KT_N)

        @block.vector
        def _(dve):
            own = Own(dve, dve_own, dve_apart)

            def split_low(phase):
                for k in range(KT_N):
                    dve.wait_ge(mvh_done, KT_N * phase + k + 1)
                    dve.tensor_tensor(mv_lo[:, k, :], Rt[:, k, :], mv_hi[:, k, :].bitcast(f32), ALU.subtract) \
                        .then_inc(mv_ready, 1)

            dve.wait_ge(mv_in[0], 16)
            split_low(0)

            def soft_in(mix, j, t):
                hh, i = STEPS[t]
                w, step = width(mix, i), STEP_BASE[mix] + NS * j + t
                buf, bank = s_sb[t % 2], s_bank[t % 2]
                dve.wait_ge(s_full, step + 1)
                if t >= 2:
                    dve.wait_ge(t_full, t_use(mix, j, ("t", t - 2), 1))
                if i == "sample":
                    dve.scalar_tensor_tensor(buf[:, 0:P], bank[:, 0:P], SCALE, bs_t[:, hh, 0:P], ALU.mult, ALU.add)
                    dve.scalar_tensor_tensor(buf[:, P:2 * P], bank[:, P:2 * P], SCALE, bmask, ALU.mult, ALU.add) \
                        .then_inc(s_taken, 1)
                    dve.wait_ge(s_taken, step + 1)
                    new = buf[:, P:2 * P].rearrange("p (b t) -> p b t", b=DEC_B)
                    own.done(dve.tensor_tensor(new, new, bs_t[:, hh, P:P + DEC_T].unsqueeze(1)
                                               .to_broadcast([P, DEC_B, DEC_T]), ALU.add))
                    own.wait()
                else:
                    dve.scalar_tensor_tensor(buf[:, 0:w], bank[:, 0:w], SCALE, bp_t[:, hh, 512 - P * (w // P):512]
                                             if mix == "b" else bp_t[:, hh, 384 - P * i:512], ALU.mult, ALU.add) \
                        .then_inc(s_taken, 1)
                    dve.wait_ge(s_taken, step + 1)
                if mix == "a":
                    dve.tensor_reduce(nmax[t % 2], buf[:, 0:w], AX.X, ALU.max, negate=True).then_inc(nmax_ready, 1)
                else:
                    own.done(dve.tensor_reduce(mx[t % 2], buf[:, 0:w], AX.X, ALU.max))
                    own.wait()
                    dve.tensor_scalar(nmax[t % 2], mx[t % 2], sinkt[:, ds(2 * j + hh, 1)], -1.0, ALU.max, ALU.mult) \
                        .then_inc(nmax_ready, 1)

            def soft_out(mix, j, t):
                w = width(mix, STEPS[t][1])
                dve.wait_ge(e_ready, STEP_BASE[mix] + NS * j + t + 1)
                total = rsum[t % 2]
                if mix == "b":
                    own.done(dve.tensor_tensor(den[t % 2], rsum[t % 2], esink[t % 2], ALU.add))
                    own.wait()
                    total = den[t % 2]
                own.done(dve.reciprocal(rden[t % 2], total))
                own.wait()
                dve.tensor_scalar(s_sb[t % 2][:, 0:w], s_sb[t % 2][:, 0:w], rden[t % 2], None, ALU.mult) \
                    .then_inc(p_ready, 1)

            def out_take(mix, j, t, pair):
                hh, i = STEPS[t]
                rows, at = slice(HD * hh, HD * hh + HD), SEQ if i == "sample" else P * i
                if t == 0:
                    dve.wait_ge(y_stored, 16 * pair)
                dve.wait_ge(o_full, STEP_BASE[mix] + NS * j + t + 1)
                dve.tensor_copy(y_t[rows, at:at + P], o_bank[rows, 0:P]).then_inc(o_taken, 1)

            dve.wait_ge(const_in, 64)
            for mix in "ab":
                with dve.Fori(0, PAIRS) as j:
                    own.enter(j, 2 + NS * (1 if mix == "a" else 3))
                    dve.wait_ge(att_in, IN_BASE[mix] + IN_PER[mix] * j + IN_PER[mix])
                    for t in range(NS + 2):
                        if t < NS:
                            soft_in(mix, j, t)
                        if 1 <= t <= NS:
                            soft_out(mix, j, t - 1)
                        if t >= 2:
                            out_take(mix, j, t - 2, j + (PAIRS if mix == "b" else 0))
                    own.leave(PAIRS)

            split_low(1)
            dve.sem_inc(z_taken, 2)
            dve.sem_inc(msum_done, 2)
            with dve.Fori(0, N_PROJ // 2) as i:
                for s in range(2):
                    m = 2 * i + s
                    ga, gb = gate_t[s][:, 0:T], gate_t[s][:, T:2 * T]
                    dve.wait_ge(sig_done, m + 1)
                    dve.wait_ge(za_done, m + 1)
                    dve.tensor_tensor(two(ga), acc(0), two(ga), ALU.mult).then_inc(z_taken, 1)
                    dve.wait_ge(unit_done, U_PROJ + m + 1)
                    dve.tensor_tensor(two(gb), acc(1), two(gb), ALU.mult).then_inc(z_taken, 1)
                    dve.wait_ge(z_taken, 2 * m + 4)
                    dve.wait_ge(m_stored[s], 16 * i)
                    dve.tensor_tensor(ev[s], ga, gb, ALU.add).then_inc(msum_done, 1)

            split_low(2)
            dve.sem_inc(r_done, 2)
            with dve.Fori(0, N_OUT // 2) as i:
                for s in range(2):
                    m = 2 * i + s
                    dve.wait_ge(x_in[s], 16 * i + 16)
                    dve.wait_ge(unit_done, U_OUT + m + 1)
                    dve.scalar_tensor_tensor(two(R[:, ds(T * m, T)]), two(x_res[s]), ALPHA, acc(s), ALU.mult, ALU.add) \
                        .then_inc(r_done, 1)

            def layer_norm(q):
                wide = [(cols, [out(z) for z in range(2)]) for (src, cols, out) in ln_parts[q]]
                dve.wait_ge(ln[q]["sum"], 1)
                for cols, out in wide:
                    last = dve.tensor_scalar(mean_t[:, cols], out[0], 1.0 / D, None, ALU.mult)
                own.done(last)
                own.wait()
                parts = ln_parts[q] if q else [(lambda k: Rt[:, k, :], slice(0, T), None)]
                for k in range(KT_N):
                    for (src, cols, _) in parts:
                        last = dve.tensor_tensor(src(k), src(k), mean_t[:, cols], ALU.subtract)
                    last.then_inc(ln[q]["centered"], 1)
                dve.wait_ge(ln[q]["sq_used"], KT_N)
                for cols, out in wide:
                    last = dve.tensor_scalar(rstd_t[:, cols], out[1], 1.0 / D, EPS, ALU.mult, ALU.add)
                last.then_inc(ln[q]["var"], 1)
                dve.wait_ge(ln[q]["std"], 1)
                own.done(dve.reciprocal(rstd_t, rstd_t))
                own.wait()
                dve.wait_ge(ln[q]["centered"], KT_N)
                for k in range(KT_N):
                    for (src, cols, _) in parts:
                        last = dve.tensor_tensor(src(k), src(k), rstd_t[:, cols], ALU.mult)
                    last.then_inc(ln[q]["scaled"], 1)

            layer_norm(0)
            split_low(3)

            def top16(n, src, alt, out_v, out_i):
                for b in range(NB):
                    last = dve.max(out_v(b)[:, 0:8], src(b))
                own.done(last)
                own.wait_apart()
                for b in range(NB):
                    dve.max_index(out_i(b)[:, 0:8], out_v(b)[:, 0:8], src(b))
                    last = dve.match_replace(alt(b), out_v(b)[:, 0:8], src(b), -3e38)
                own.done(last)
                own.wait_apart()
                for b in range(NB):
                    last = dve.max(out_v(b)[:, 8:16], alt(b))
                own.done(last)
                own.wait_apart()
                for b in range(NB):
                    last = dve.max_index(out_i(b)[:, 8:16], out_v(b)[:, 8:16], alt(b))
                return last

            dve.sem_inc(topk_done, 2)
            cand4 = cand.rearrange("p (b i j) -> p b i j", b=NB, i=TOPK)
            eq3 = eq.rearrange("p (n k) -> p n k", k=TOPK)
            eq4 = eq.rearrange("p (b n k) -> p b n k", b=NB, n=TOPK)
            full = [P, NB, TOPK, TOPK]
            with dve.Fori(0, N_QUERY // 2) as i:
                own.enter(i, 6 + 1 + 3 + 1 + 2 + 6)
                for s in range(2):
                    dve.wait_ge(sc_taken, 2 * i + s + 3)
                    dve.sem_inc(dve_apart, 1)
                    top16(KEYS, lambda b: sc_sb[s][:, P * b:P * b + P], lambda b: sc2[:, P * b:P * b + P],
                          lambda b: val[:, b, s, :], lambda b: idx_u[:, b, s, :]).then_inc(topk_done, 1)
                dve.wait_ge(topk_done, 2 * i + 4)
                dve.tensor_copy(idx_f, idx_u)
                own.done(dve.tensor_tensor(cand4, val[:, :, 0, :].unsqueeze(3).to_broadcast(full),
                                           val[:, :, 1, :].unsqueeze(2).to_broadcast(full), ALU.add))
                own.wait_apart()
                own.done(top16(TOPK * TOPK, lambda b: cand[:, 256 * b:256 * b + 256], lambda b: cand2[:, 256 * b:256 * b + 256],
                               lambda b: top_v[:, TOPK * b:TOPK * b + TOPK], lambda b: ci_u[:, TOPK * b:TOPK * b + TOPK]))
                own.wait()
                dve.tensor_copy(pick_g[:, :, ds(TOPK * i, TOPK)], top_v.rearrange("p (b k) -> p b k", b=NB))
                dve.tensor_scalar(cp_u[0], ci_u, 4, None, ALU.logical_shift_right)
                own.done(dve.tensor_scalar(cp_u[1], ci_u, TOPK - 1, None, ALU.bitwise_and))
                own.wait()
                dve.tensor_copy(c_f[0], cp_u[0])
                own.done(dve.tensor_copy(c_f[1], cp_u[1]))
                own.wait()
                for z in range(2):
                    own.done(dve.tensor_tensor(eq3, c_f[z].unsqueeze(2).to_broadcast([P, NB * TOPK, TOPK]),
                                               iota[:, 0:TOPK].unsqueeze(1).to_broadcast([P, NB * TOPK, TOPK]),
                                               ALU.is_equal))
                    own.wait()
                    own.done(dve.tensor_tensor(eq4, eq4, idx_f[:, :, z, :].unsqueeze(2).to_broadcast(full), ALU.mult))
                    own.wait()
                    own.done(dve.tensor_reduce(pick_e[z][:, :, ds(TOPK * i, TOPK)], eq4, AX.X, ALU.add))
                    own.wait()
                own.leave(N_QUERY // 2)

            g3 = pick_g.rearrange("p b (h k) -> p (b h) k", k=TOPK)
            own.wait()
            gm = cand[:, 0:NB * PH]
            own.done(dve.tensor_copy(gm.unsqueeze(2), g3[:, :, 0:1]))
            own.wait()
            wide = [P, NB * PH, TOPK]
            dve.tensor_tensor(g3, g3, gm.unsqueeze(2).to_broadcast(wide), ALU.subtract).then_inc(gexp_in, 1)
            dve.wait_ge(gexp_done, 1)
            own.done(dve.tensor_reduce(psum_g, g3, AX.X, ALU.add))
            own.wait()
            own.done(dve.reciprocal(psum_g, psum_g))
            own.wait()
            dve.tensor_tensor(g3, g3, psum_g.unsqueeze(2).to_broadcast(wide), ALU.mult).then_inc(picks_done, 1)
            dve.wait_ge(picks_done, 1)
            dve.tensor_copy(gate_n, pick_g[:, NB - 1, :])
            dve.scalar_tensor_tensor(idx_n, pick_e[0][:, NB - 1, :], float(KEYS), pick_e[1][:, NB - 1, :],
                                     ALU.mult, ALU.add).then_inc(idx_ready, 1)

            dve.wait_ge(picks_taken, 3)
            with dve.Fori(0, GBLK // 2) as i:
                for q in range(2 * GT // 4):
                    dve.wait_ge(g_full, 16 * i + q + 1)
                    for t in range(4):
                        n = 4 * (q % 2) + t
                        tok = ds(2 * GT * i + 4 * q + t, 1)
                        dve.tensor_scalar(oh2[:, n, :], iota, pick_t[2][:, tok], None, ALU.is_equal)
                        last = dve.tensor_scalar(oh1[:, n, :], iota, pick_t[1][:, tok], pick_t[0][:, tok],
                                                 ALU.is_equal, ALU.mult)
                    last.then_inc(oh_ready, 1)

            for w in range(2):
                dve.wait_ge(g_stored[w], 16 * (GBLK // 2))
            dve.wait_ge(nat_ready, 1)
            dve.memset(R[:, 0:KT_N * SEQ], 0.0).then_inc(out_evac, 1)
            dve.wait_ge(out_evac, 1)
            dve.sem_inc(out_evac, 3)
            dve.sem_inc(w_ready, 2)
            dve.sem_inc(rows_used, 2)

            def gather_step(table, g, c):
                rows = rows_t[c % 2]
                dve.wait_ge(rows_in[c % 2], 16 * (STEPS_G // 2 * g + c // 2 + 1))
                if table == "u":
                    ins = dve.tensor_tensor_reduce(rows, rows, nat, 1.0, 0.0, ALU.mult, ALU.add, dots[:, c:c + 1])
                else:
                    dve.wait_ge(rows_used, STEPS_G * g + c + 2)
                    w = act_n[:, ds(STEPS_G * (g - GROUPS // 2) + c, 1)]
                    ins = dve.scalar_tensor_tensor(nat, rows, w, nat, ALU.mult, ALU.add)
                ins.then_inc(rows_used, 1)
                if table == "u" and c == STEPS_G - 1:
                    dve.wait_ge(rows_used, STEPS_G * g + c + 3)
                    own.done(dve.tensor_copy(act_n[:, ds(STEPS_G * g, STEPS_G)], dots[:, :]))
                    own.wait()

            def product(g, e):
                a3 = act_t[e % 2].rearrange("p (b t) -> p b t", b=GBLK)
                dve.tensor_tensor(a3, a3, G4[:, :, e, :], ALU.mult).then_inc(w_prod, 1)
                dve.wait_ge(wwh_done, 4 * g + e + 1)
                dve.tensor_tensor(ww_lo[:, e, :], act_t[e % 2], ww_hi[:, e, :].bitcast(f32), ALU.subtract) \
                    .then_inc(w_ready, 1)

            def add_out(g, v, first):
                for d in range(4):
                    dt = 4 * v + d
                    if d < 3:
                        dve.wait_ge(part_done, 12 * g + 3 * v + d + 1)
                    else:
                        dve.wait_ge(unit_done, first + v + 1)
                    dve.tensor_tensor(r_acc[:, dt, :], r_acc[:, dt, :], banks[:, dt % 4, :], ALU.add) \
                        .then_inc(out_evac, 1)

            with dve.Fori(0, EARLY) as g:
                own.enter(g, 1)
                dve.wait_ge(g4_in, 16 * g + 16)
                for e in range(EG):
                    dve.wait_ge(act_in[e % 2], 16 * (2 * g + e // 2 + 1))
                    product(g, e)
                for v in range(EG):
                    gather_step("u", g, 2 * v)
                    gather_step("u", g, 2 * v + 1)
                    add_out(g, v, U_PEER + N_EARLY + EG * g)
                own.leave(EARLY)

            def main_group(table, g):
                dve.wait_ge(g4_in, 16 * g + 16)
                for e in range(EG):
                    gather_step(table, g, e)
                    dve.wait_ge(gelu_done, 4 * g + e + 1)
                    product(g, e)
                for v in range(EG):
                    gather_step(table, g, EG + v)
                    add_out(g, v, U_PEER + 8 * g + EG)

            with dve.Fori(EARLY, GROUPS // 2) as g:
                own.enter(g - EARLY, 1)
                main_group("u", g)
                own.leave(GROUPS // 2 - EARLY)
            own.wait()
            own.done(dve.memset(nat, 0.0))
            own.wait()
            dve.sem_inc(act_n_ready, 1)
            dve.wait_ge(act_n_gelu, 1)
            own.done(dve.tensor_tensor(act_n, act_n, gate_n, ALU.mult))
            own.wait()
            with dve.Fori(GROUPS // 2, GROUPS) as g:
                main_group("v", g)

            dve.wait_ge(rows_used, 2 + STEPS_G * GROUPS)
            dve.tensor_copy(rows_t[0], nat).then_inc(nat_out, 1)
            dve.wait_ge(out_evac, 4 + KT_N * GROUPS)
            dve.wait_ge(smp_ready, 1)
            for part in (mv_hi, mv_lo):
                own.done(dve.scalar_tensor_tensor(r_smp, part[:, :, SEQ:T].bitcast(f32), ALPHA, r_smp, ALU.mult, ALU.add))
                own.wait()
            for k in range(KT_N):
                for part in (mv_hi, mv_lo):
                    last = dve.scalar_tensor_tensor(r_acc[:, k, :], part[:, k, 0:SEQ].bitcast(f32), ALPHA, r_acc[:, k, :],
                                                    ALU.mult, ALU.add)
                    if part is mv_hi:
                        own.done(last)
                        own.wait()
                last.then_inc(res_done, 1)
            dve.wait_ge(res_done, KT_N)
            layer_norm(1)


def kernel(**inputs):
    import concourse.bacc as _bacc
    from concourse import mybir as _mybir
    from concourse.bass_utils import run_bass_kernel_spmd as _run

    a = {k: np.asarray(v) for k, v in inputs.items()}
    f = np.float32
    x = np.concatenate([a["x_prompt"].reshape(SEQ, D), a["x_sample"].reshape(-1, D)], 0)
    x_t = np.ascontiguousarray(x.T).reshape(KT_N, P, T)

    order = np.array([h for j in range(PAIRS) for h in (j, PAIRS + j)])

    def units(w):
        rows, cols = w.shape
        return w.reshape(rows // P, P, cols // P, P).transpose(2, 1, 0, 3).reshape(cols // P, P, rows)

    w_in = a["w_in"]
    cut = np.cumsum([0, 1024, 1024, 1024, 1024, 128, 128, 2048, 2048])
    qa, ka, va, qb, kb, vb, ga, gb = (w_in[:, cut[i]:cut[i + 1]] for i in range(8))
    qb = qb.reshape(D, 16, HD)[:, order].reshape(D, 1024)
    wpb = a["w_proj_b"].reshape(16, HD, D)[order].reshape(1024, D)
    ws = np.empty((UNITS, P, D), f)
    ws[U_QKV:U_GATE] = np.concatenate([units(w) for w in (ka, va, kb, vb, qa, qb)], 0)
    ws[U_GATE:U_PROJ:2] = units(ga)
    ws[U_GATE + 1:U_PROJ:2] = units(gb)
    ws[U_PROJ:U_OUT] = units(np.concatenate([a["w_proj_a"], wpb], 0))
    ws[U_OUT:U_QUERY] = units(a["w_out"])
    ws[U_QUERY:U_PEER] = units(a["peer_w_query"])
    u = a["peer_u"].reshape(GROUPS, EG, KEYS, KT_N, P).transpose(0, 1, 4, 3, 2).reshape(GROUPS, EG, P, D)
    v = a["peer_v"].reshape(GROUPS, EG, KEYS, 4, 4, P).transpose(0, 3, 2, 4, 1, 5).reshape(GROUPS, EG, P, D)
    ws[U_PEER:U_PEER + N_EARLY] = u[:EARLY].reshape(-1, P, D)
    ws[U_PEER + N_EARLY:U_PEER + 2 * N_EARLY] = v[:EARLY].reshape(-1, P, D)
    late = ws[U_PEER + 2 * N_EARLY:].reshape(GROUPS - EARLY, 2, EG, P, D)
    late[:, 0], late[:, 1] = u[EARLY:], v[EARLY:]

    cka = a["cache_a_k"].reshape(DEC_B, PAST, PAIRS, 2 * HD).transpose(2, 3, 0, 1).reshape(PAIRS, P, DEC_B * PAST)
    cva = a["cache_a_v"].reshape(DEC_B, PAST, PAIRS, 2 * HD).transpose(2, 1, 0, 3).reshape(PAIRS, P, DEC_B * P)
    ckb = a["cache_b_k"].reshape(DEC_B, PAST, 2 * HD).transpose(2, 0, 1).reshape(P, DEC_B * PAST)
    cvb = a["cache_b_v"].reshape(DEC_B, PAST, 2 * HD).transpose(1, 0, 2).reshape(P, DEC_B * P)

    rext = np.pad(a["rel_bias_table"], ((0, 0), (0, 383)), mode="edge")[:, ::-1]
    negs = np.full((16, 64, 64), NEG, f)
    slope = np.exp2(-8.0 * np.arange(1, 17) / 16).astype(f)[order]
    q, c = np.arange(P)[:, None], np.arange(256)[None]
    seen = (q + P) // 64 - c // 64
    bp_b = np.where((seen >= 0) & (seen <= 2), -slope[:, None, None] * np.abs(q + P - c).astype(f), f(NEG)).astype(f)
    bs_b = (-slope[:, None, None] * np.abs(q % DEC_T + PAST - np.arange(144)[None]).astype(f)).astype(f)
    bmask = np.where(q // DEC_T == np.arange(P)[None] // DEC_T, f(0), f(NEG))
    consts = np.concatenate([np.eye(P), np.ones((P, P)), np.tile(np.arange(P), (P, 1)), bmask], 1).astype(f)
    sinks = np.tile(a["b_sinks"][order][None], (P, 1))
    lnp = np.concatenate([a[n].reshape(KT_N, P).T for n in ("ln1_g", "ln1_b", "ln2_g", "ln2_b")], 1)
    subk = np.concatenate([a["peer_sub_keys_1"].T, a["peer_sub_keys_2"].T], 1)

    nc = _bacc.Bacc("TRN2", target_bir_lowering=False, num_devices=1)
    arrays, args = {}, []
    for name, arr in (("x_t", x_t), ("wstream", ws), ("u_rows", a["peer_u"]), ("v_rows", a["peer_v"]), ("cka", cka), ("cva", cva), ("ckb", ckb), ("cvb", cvb),
                      ("rext", rext), ("negs", negs), ("bp_b", bp_b), ("bs_b", bs_b), ("sinks", sinks), ("lnp", lnp),
                      ("subk", subk), ("consts", consts)):
        arrays["in_" + name] = np.ascontiguousarray(arr)
        args.append(nc.dram_tensor("in_" + name, arr.shape, _mybir.dt.from_np(arr.dtype), kind="ExternalInput").ap())
    args.append(nc.dram_tensor("out_p", (N_QKV, P, T), _mybir.dt.float32, kind="ExternalOutput").ap())
    args.append(nc.dram_tensor("out_y", (KT_N, P, T), _mybir.dt.float32, kind="ExternalOutput").ap())
    build(nc, *args)
    r = _run(nc, [arrays], core_ids=[0]).results[0]
    p = np.asarray(r["out_p"])
    y = np.asarray(r["out_y"]).reshape(D, T).T

    def heads(lo, n):
        return np.ascontiguousarray(p[lo:lo + n].reshape(n * P, T).T).reshape(T, n * 2, HD)

    k_a, v_a, k_b, v_b = heads(0, 8), heads(8, 8), heads(16, 1), heads(17, 1)
    prompt = lambda t, n: np.ascontiguousarray(t[SEQ - n:SEQ])[None]
    sample = lambda t: np.ascontiguousarray(t[SEQ:]).reshape((DEC_B, DEC_T) + t.shape[1:])
    return (np.ascontiguousarray(y[:SEQ])[None], np.ascontiguousarray(y[SEQ:]).reshape(DEC_B, DEC_T, D),
            prompt(k_a, SEQ), prompt(v_a, SEQ), prompt(k_b, 128), prompt(v_b, 128),
            sample(k_a), sample(v_a), sample(k_b), sample(v_b))
```

```python
from contextlib import ExitStack

import numpy as np
import concourse.bass as bass
from concourse import mybir

P = 128
D = 2048
KT_N = D // P
SEQ, DEC_B, DEC_T = 512, 8, 16
T = SEQ + DEC_B * DEC_T
HALF = T // 2
NB = T // P
PAST = 128
HD = 64
PAIRS = 8
PH, TOPK, KEYS = 8, 16, 128
EPS = 1e-5
ALPHA = float(2.0 ** 0.25)
SCALE = HD ** -0.5
NEG = -1e30
EG = 4
GROUPS = KEYS // EG
GT = 32
GBLK = SEQ // GT
TAIL = 8
TAIL_PICKS = 6
EARLY = 6
N_EARLY = EG * EARLY
PICKS = PH * TOPK
STEPS_G = 2 * PICKS // GROUPS
MIXED_STEPS = [[0], [1], [2], [3], [4, 5], [6], [7], [8, 9], [10], [11, 12], [13], [14, 15]]

N_QKV, N_GATE, N_PROJ, N_OUT, N_QUERY = 34, 32, 16, 16, 16
U_QKV = 0
U_GATE = U_QKV + N_QKV
U_PROJ = U_GATE + N_GATE
U_OUT = U_PROJ + N_PROJ
U_QUERY = U_OUT + N_OUT
U_PEER = U_QUERY + N_QUERY
UNITS = U_PEER + 2 * EG * GROUPS
ROW_KB, ROW_QA, ROW_QB = 16, 18, 26


class Own:

    def __init__(self, eng, sem, apart):
        self.eng, self.sem, self.apart, self.n, self.off = eng, sem, apart, 0, 0

    def done(self, ins):
        ins.then_inc(self.sem, 1)
        self.n += 1

    def wait(self):
        self.eng.wait_ge(self.sem, self.off + self.n)

    def wait_apart(self):
        self.wait()
        self.eng.sem_inc(self.apart, 1)

    def enter(self, i, per):
        self.start, self.per = self.n, per
        self.off = i * per

    def leave(self, trips):
        assert self.n - self.start == self.per, (self.n - self.start, self.per)
        self.n, self.off = self.start + self.per * trips, 0


def build(nc, x_t, wstream, u_rows, v_rows, cka, cva, ckb, cvb, rext, negs, bp_b, bs_b, sinks, lnp, subk, consts, pt_out, y_out):
    f32, f32r, u32 = mybir.dt.float32, mybir.dt.float32r, mybir.dt.uint32
    ALU, ACT = mybir.AluOpType, mybir.ActivationFunctionType
    AX = mybir.AxisListType
    ds = bass.ds

    with ExitStack() as ctx:
        def dram(name, shape):
            return nc.dram_tensor(name, shape, f32).ap()

        def sb(name, shape, dt=f32):
            return ctx.enter_context(nc.sbuf_tensor(name, shape, dt))

        def sem(name):
            return ctx.enter_context(nc.semaphore(name))

        g_s = dram("gate_scratch", (N_GATE, P, T))
        y_s = dram("attn_scratch", (KT_N, P, T))
        bp_a = dram("bias_prompt_a", (16, P, 512))
        bs_a = dram("bias_sample_a", (16, P, 144))
        a_s = dram("early_act", (N_EARLY, P, SEQ))
        G_s = dram("gate_matrix", (GBLK, P, KEYS, GT))

        raw = [sb(f"w_raw{s}", [P, D]) for s in range(2)]
        w_hi = [sb(f"w_hi{s}", [P, D], f32r) for s in range(2)]
        w_lo = [sb(f"w_lo{s}", [P, D], f32r) for s in range(2)]
        mv_hi = sb("mv_hi", [P, KT_N, T], f32r)
        mv_lo = sb("mv_lo", [P, KT_N, T], f32r)
        R = sb("work", [P, KT_N * T])
        ww_hi = sb("ww_hi", [P, EG, SEQ], f32r)
        ww_lo = sb("ww_lo", [P, EG, SEQ], f32r)
        W2 = sb("work2", [P, 5120])
        idx2 = sb("idx2", [P, 2], u32)
        cst = sb("cst", [P, 4 * P])
        subkt = sb("subkt", [P, 2 * KEYS])
        sinkt = sb("sinkt", [P, 16])
        lnt = sb("lnt", [P, 4 * KT_N])
        small = sb("small", [P, 16])

        ident, ones, iota, bmask = (cst[:, P * i:P * i + P] for i in range(4))
        Rt = R[:, :].rearrange("p (k t) -> p k t", k=KT_N)

        def area(at, n):
            return R[:, at:at + n]
        ck_t, cv_t = area(0, 1024), area(1024, 1024)
        bp_t = area(2048, 1024).rearrange("p (h c) -> p h c", h=2)
        bs_t = area(3072, 288).rearrange("p (h c) -> p h c", h=2)
        q_t, k_t, v_t = area(3360, T), area(4000, T), area(4640, T)
        vn = area(5280, T)
        s_sb = [area(5920, 512), area(6432, 512)]
        pt_sb = [area(6944, 512), area(7456, 512)]
        st_both = area(7968, 2 * P)
        st_sb = [st_both[:, 0:P], st_both[:, P:2 * P]]
        y_t = area(8224, T)
        vn_b, v_b = area(8864, T), area(9504, T)
        mx = [small[:, s:s + 1] for s in range(2)]
        nmax = [small[:, 2 + s:3 + s] for s in range(2)]
        rsum = [small[:, 4 + s:5 + s] for s in range(2)]
        esink = [small[:, 6 + s:7 + s] for s in range(2)]
        rden = [small[:, 8 + s:9 + s] for s in range(2)]
        den = [small[:, 10 + s:11 + s] for s in range(2)]

        ev = [W2[:, T * s:T * s + T] for s in range(2)]
        gate_t = [W2[:, 2 * T * (s + 1):2 * T * (s + 2)] for s in range(2)]
        q_both = W2[:, 2 * T:2 * T + 2 * P].rearrange("p (b h t) -> p b h t", b=DEC_B, h=2)
        x_res = [W2[:, 2 * T + T * s:3 * T + T * s] for s in range(2)]
        lsum = W2[:, 4 * T:5 * T]
        psum = W2[:, SEQ:2 * SEQ]
        mean_t, rstd_t = W2[:, 0:T], W2[:, T:2 * T]
        sq_t = x_res
        act_t = [W2[:, SEQ * s:SEQ * s + SEQ] for s in range(2)]
        pick_t = [W2[:, SEQ * (q + 2):SEQ * (q + 3)] for q in range(3)]
        oh1 = W2[:, 5 * SEQ:5 * SEQ + 8 * P].rearrange("p (n e) -> p n e", n=8)
        oh2 = ww_hi[:, :, :].rearrange("p e t -> p (e t)")[:, 0:8 * P].rearrange("p (n e) -> p n e", n=8)
        G4 = W2[:, 2 * SEQ:6 * SEQ].rearrange("p (b e t) -> p b e t", b=GBLK, e=EG)
        r_acc = R[:, 0:KT_N * SEQ].rearrange("p (k t) -> p k t", k=KT_N)
        r_smp = R[:, KT_N * SEQ:KT_N * T].rearrange("p (k t) -> p k t", k=KT_N)
        rows_t = [W2[:, 6 * SEQ:10 * SEQ], R[:, KT_N * SEQ:KT_N * T]]
        gate_n, idx_n, act_n = cst[:, 3 * P:4 * P], subkt[:, 0:P].bitcast(u32), subkt[:, P:2 * P]
        dots = sb("dots", [P, STEPS_G])

        qe = [area(0, T), area(T, T)]
        sc_sb = [area(1280, T), area(1920, T)]
        sc2 = area(2560, T)
        cand, cand2 = area(3200, 1280), area(4480, 1280)
        val = area(5760, 160).rearrange("p (b s k) -> p b s k", b=NB, s=2)
        idx_f = area(5920, 160).rearrange("p (b s k) -> p b s k", b=NB, s=2)
        pick_g = area(6080, T).rearrange("p (b k) -> p b k", b=NB)
        c_f = [area(6720, 80), area(6800, 80)]
        eq = area(6880, 1280)
        pick_e = [area(8160, T).rearrange("p (b k) -> p b k", b=NB), area(8800, T).rearrange("p (b k) -> p b k", b=NB)]
        idx_u = area(9440, 160).bitcast(u32).rearrange("p (b s k) -> p b s k", b=NB, s=2)
        ci_u = area(9600, 80).bitcast(u32)
        cp_u = [area(9680, 80).bitcast(u32), area(9760, 80).bitcast(u32)]
        psum_g = area(9840, 40)
        top_v = area(9880, 80)
        g_buf = [area(w * GT * KEYS, GT * KEYS).rearrange("p (e t) -> p e t", t=GT) for w in range(2)]

        banks = ctx.enter_context(nc.psum_tensor("banks", [P, 8, 512], f32))

        def acc(s):
            return banks[:, 2 * s:2 * s + 2, 0:HALF]

        nat = banks[:, 4:8, :].rearrange("p b c -> p (b c)")

        def two(ap):
            return ap.rearrange("p (a t) -> p a t", a=2)

        s_bank = [banks[:, 4, :], banks[:, 5, :]]
        t_bank, o_bank = banks[:, 6, :], banks[:, 7, :]

        ln_parts = [[(lambda k, h=h: Rt[:, k, HALF * h:HALF * h + HALF], slice(HALF * h, HALF * h + HALF),
                      lambda z, h=h: acc(z)[:, h, :]) for h in range(2)],
                    [(lambda k: r_acc[:, k, :], slice(0, SEQ), lambda z: banks[:, 2 * z, 0:SEQ]),
                     (lambda k: r_smp[:, k, :], slice(SEQ, T), lambda z: banks[:, 2 * z + 1, 0:T - SEQ])]]

        def sc_parts(s):
            return banks[:, 4 + 2 * s, :], banks[:, 5 + 2 * s, 0:P]

        raw_full = [sem(f"raw_full{s}") for s in range(2)]
        hi_done, split_done, unit_done = sem("hi_done"), sem("split_done"), sem("unit_done")
        mv_in = [sem(f"mv_in{q}") for q in range(KT_N // 2)]
        mvh_done, mv_ready = sem("mvh_done"), sem("mv_ready")
        const_in, tab_done = sem("const_in"), sem("tab_done")
        qkv_evac, gate_evac = sem("qkv_evac"), sem("gate_evac")
        qkv_stored = [sem(f"qkv_stored{s}") for s in range(2)]
        gate_stored = [sem(f"gate_stored{s}") for s in range(2)]
        att_v_b, q_both_ready = sem("att_v_b"), sem("q_both_ready")
        att_q, att_b, att_c = sem("att_q"), sem("att_b"), sem("att_c")
        s_full, s_taken, nmax_ready, e_ready, p_ready = (
            sem(n) for n in ("s_full", "s_taken", "nmax_ready", "e_ready", "p_ready"))
        t_full, t_taken, o_full, o_taken, y_stored = (
            sem(n) for n in ("t_full", "t_taken", "o_full", "o_taken", "y_stored"))
        gate_in = [sem(f"gate_in{s}") for s in range(2)]
        sig_done, za_done, z_taken, msum_done = (sem(n) for n in ("sig_done", "za_done", "z_taken", "msum_done"))
        x_in = [sem(f"x_in{s}") for s in range(2)]
        r_done = sem("r_done")
        ln = [{n: sem(f"ln{p}_{n}") for n in ("sum", "centered", "squared", "sq_used", "var", "std", "scaled", "out")}
              for p in range(2)]
        y_out_done = sem("y_out_done")
        lsum_done = sem("lsum_done")
        psum_done = sem("psum_done")
        q_evac, sc_full, sc_taken, topk_done = (sem(n) for n in ("q_evac", "sc_full", "sc_taken", "topk_done"))
        gexp_in, gexp_done, picks_done, picks_full, picks_taken = (
            sem(n) for n in ("gexp_in", "gexp_done", "picks_done", "picks_full", "picks_taken"))
        oh_ready, g_full, g_evac = sem("oh_ready"), sem("g_full"), sem("g_evac")
        act_stored = [sem(f"act_stored{s}") for s in range(2)]
        act_in = [sem(f"act_in{s}") for s in range(2)]
        rows_in = [sem(f"rows_in{s}") for s in range(2)]
        idx_ready, idx2_ready, rows_used, nat_ready, act_n_ready, act_n_gelu, nat_out, nat_t, smp_ready = (
            sem(n) for n in ("idx_ready", "idx2_ready", "rows_used", "nat_ready", "act_n_ready", "act_n_gelu",
                             "nat_out", "nat_t", "smp_ready"))
        g_stored = [sem(f"g_stored{w}") for w in range(2)]
        g4_in, gelu_done, w_prod, wwh_done, w_ready, part_done, out_evac = (
            sem(n) for n in ("g4_in", "gelu_done", "w_prod", "wwh_done", "w_ready", "part_done", "out_evac"))
        dve_own = sem("dve_own")
        dve_apart, pool_apart = sem("dve_apart"), sem("pool_apart")

        STEPS = [(hh, i) for hh in range(2) for i in range(4)] + [(0, "sample"), (1, "sample")]
        NS = len(STEPS)

        def width(mix, i):
            if i == "sample":
                return 2 * P
            return P * (i + 1) if mix == "a" else P * min(i + 1, 2)

        T_USES = {m: ([("v", 0), ("v", 1)] if m == "a" else [])
                  + [("t", t) for t in range(6)] + [("c", 0)] + [("t", t) for t in range(6, NS)]
                  for m in "ab"}
        T_BASE = {"a": 2, "b": 2 + len(T_USES["a"]) * PAIRS}
        STEP_BASE = {"a": 0, "b": NS * PAIRS}
        Q_BASE, Q_PER = {"a": 0, "b": 16 * (3 * PAIRS + 1)}, {"a": 16 * 3, "b": 16}
        BIAS_BASE = {"a": 0, "b": 16 * 2 * PAIRS}

        def t_use(mix, j, what, extra=0):
            return T_BASE[mix] + j * len(T_USES[mix]) + T_USES[mix].index(what) + extra

        block = ctx.enter_context(nc.Block())

        @block.sync
        def _(sp):
            for s in range(2):
                sp.dma_start(raw[s][:, :], wstream[s]).then_inc(raw_full[s], 16)
            with sp.Fori(1, UNITS // 2) as i:
                for s in range(2):
                    sp.wait_ge(split_done, 2 * i + s - 1)
                    sp.dma_start(raw[s][:, :], wstream[ds(2 * i + s, 1)].rearrange("a p c -> p (a c)")) \
                        .then_inc(raw_full[s], 16)

        @block.gpsimd
        def _(pool):
            def split(s, pair):
                pool.wait_ge(raw_full[s], 16 * pair + 16)
                pool.sem_inc(pool_apart, 1)
                pool.tensor_scalar(w_hi[s][:, :], raw[s][:, :], 1.0, 0.0, ALU.mult, ALU.add).then_inc(hi_done, 1)
                pool.wait_ge(hi_done, 2 * pair + s + 1)
                pool.tensor_tensor(w_lo[s][:, :], raw[s][:, :], w_hi[s][:, :].bitcast(f32), ALU.subtract) \
                    .then_inc(split_done, 1)

            def split_next(s, pair):
                pool.wait_ge(unit_done, 2 * pair + s - 1)
                split(s, pair)

            for s in range(2):
                split(s, 0)
            with pool.Fori(1, (U_PEER + N_EARLY) // 2) as i:
                for s in range(2):
                    split_next(s, i)

            def gather(table, g, c, first=0):
                idx = idx2[:, c % 2:c % 2 + 1]
                pool.wait_ge(rows_used, STEPS_G * g + c + 1)
                pool.sem_inc(pool_apart, 1)
                pool.tensor_copy(idx, idx_n[:, ds(STEPS_G * (g - first) + c, 1)]).then_inc(idx2_ready, 1)
                pool.wait_ge(idx2_ready, STEPS_G * g + c + 1)
                pool.sem_inc(pool_apart, 1)
                pool.indirect_dma_start(rows_t[c % 2], None, table, bass.IndirectOffsetOnAxis(ap=idx, axis=0)) \
                    .then_inc(rows_in[c % 2], 16)

            pool.wait_ge(idx_ready, 1)
            with pool.Fori(0, EARLY) as i:
                for n in range(3 * EG):
                    split_next(n % 2, (U_PEER + N_EARLY) // 2 + 6 * i + n // 2)
                    for c in MIXED_STEPS[n]:
                        gather(u_rows, 2 * i + c // STEPS_G, c % STEPS_G)
            for table, lo, hi in ((u_rows, 2 * EARLY, GROUPS // 2), (v_rows, GROUPS // 2, GROUPS)):
                with pool.Fori(lo, hi) as g:
                    for n in range(2 * EG):
                        split_next(n % 2, U_PEER // 2 + EG * g + n // 2)
                        gather(table, g, n, 0 if table is u_rows else GROUPS // 2)

        @block.tensor
        def _(pe):
            for first in (s_taken, t_taken, o_taken):
                pe.sem_inc(first, 1)

            def k_step(s, k, dst, k_first, k_last, phase):
                if phase is not None and k % 2 == 0:
                    pe.wait_ge(mv_ready, KT_N * phase + k + 2)
                for n, (a, b) in enumerate(((w_hi, mv_hi), (w_hi, mv_lo), (w_lo, mv_hi))):
                    for h in range(2):
                        last = pe.matmul(acc(dst)[:, h, :], a[s][:, P * k:P * k + P], b[:, k, HALF * h:HALF * h + HALF],
                                         start=(k == k_first and n == 0), stop=(k == k_last and n == 2))
                return last

            def unit(s, n, free, phase):
                pe.wait_ge(split_done, n + 1)
                pe.wait_ge(*free)
                for k in range(KT_N):
                    last = k_step(s, k, s, 0, KT_N - 1, phase)
                last.then_inc(unit_done, 1)

            with pe.Fori(0, N_QKV // 2) as i:
                for s in range(2):
                    unit(s, U_QKV + 2 * i + s, (qkv_evac, 2 * i + s + 1), 0)

            def scores(mix, j, t):
                hh, i = STEPS[t]
                rows = slice(HD * hh, HD * hh + HD)
                bank = s_bank[t % 2]
                if t >= 1:
                    pe.wait_ge(s_taken, 1 + STEP_BASE[mix] + NS * j + t - 1)
                if i == "sample":
                    pe.wait_ge(t_taken, 1 + t_use(mix, j, ("c", 0), 1))
                    pe.transpose(bank[:, 0:P], st_sb[hh][:, :], ident)
                    last = pe.matmul(bank[:, P:2 * P], q_t[rows, SEQ:T], k_t[rows, SEQ:T], start=True, stop=True)
                else:
                    w = width(mix, i)
                    end = P * (i + 1)
                    last = pe.matmul(bank[:, 0:w], q_t[rows, P * i:end], k_t[rows, end - w:end], start=True, stop=True)
                last.then_inc(s_full, 1)

            def transpose_p(mix, j, t):
                w = width(mix, STEPS[t][1])
                pe.wait_ge(p_ready, STEP_BASE[mix] + NS * j + t + 1)
                pe.wait_ge(t_taken, 1 + t_use(mix, j, ("t", t)))
                for c in range(w // P):
                    last = pe.transpose(t_bank[:, P * c:P * c + P], s_sb[t % 2][:, P * c:P * c + P], ident)
                last.then_inc(t_full, 1)

            def cached_scores(mix, j):
                pe.wait_ge(att_c, 32 * j + 32 if mix == "a" else 32 * PAIRS + 32)
                pe.wait_ge(q_both_ready, (PAIRS if mix == "b" else 0) + j + 1)
                pe.wait_ge(t_taken, 1 + t_use(mix, j, ("c", 0)))
                for b in range(DEC_B):
                    last = pe.matmul(t_bank[:, 32 * b:32 * b + 32], ck_t[:, P * b:P * b + P],
                                     q_both[:, b, :, :], start=True, stop=True)
                last.then_inc(t_full, 1)

            def values(mix, j, t):
                hh, i = STEPS[t]
                rows, pt = slice(HD * hh, HD * hh + HD), pt_sb[t % 2]
                pe.wait_ge(t_taken, 1 + t_use(mix, j, ("t", t), 1))
                pe.wait_ge(o_taken, 1 + STEP_BASE[mix] + NS * j + t)
                o, v_nat = o_bank[rows, 0:P], vn if mix == "a" else vn_b
                if i == "sample":
                    for b in range(DEC_B):
                        c = DEC_T * b
                        pe.matmul(o[:, c:c + DEC_T], cv_t[:, P * b + HD * hh:P * b + HD * hh + HD],
                                  pt[:, c:c + DEC_T], start=(b == 0), stop=False)
                    last = pe.matmul(o, v_nat[:, P * 4 + HD * hh:P * 4 + HD * hh + HD], pt[:, P:2 * P],
                                     start=False, stop=True)
                else:
                    nk = width(mix, i) // P
                    for c in range(nk):
                        kb = i + 1 - nk + c
                        last = pe.matmul(o, v_nat[:, P * kb + HD * hh:P * kb + HD * hh + HD], pt[:, P * c:P * c + P],
                                         start=(c == 0), stop=(c == nk - 1))
                last.then_inc(o_full, 1)

            def transpose_v(first, use, src=v_t):
                pe.wait_ge(t_taken, 1 + use)
                for b in (range(4) if first else (4,)):
                    last = pe.transpose(t_bank[:, P * (b % 4):P * (b % 4) + P], src[:, P * b:P * b + P], ident)
                last.then_inc(t_full, 1)

            def attention_pair(mix, j):
                first = U_GATE + 2 * (j + (PAIRS if mix == "b" else 0))
                k_steps = [(s, k) for s in range(2) for k in range(KT_N)]

                def gemm(n):
                    for _ in range(n):
                        s, k = k_steps.pop(0)
                        if k == 0:
                            pe.wait_ge(split_done, first + s + 1)
                            pe.wait_ge(gate_evac, first - U_GATE + s + 1)
                        last = k_step(s, k, s, 0, KT_N - 1, None)
                        if k == KT_N - 1:
                            last.then_inc(unit_done, 1)

                gemm(9 if mix == "a" else 7)
                pe.wait_ge(att_q, Q_BASE[mix] + Q_PER[mix] * j + Q_PER[mix])
                if mix == "a":
                    transpose_v(True, t_use(mix, j, ("v", 0)))
                gemm(2 if mix == "a" else 1)
                if mix == "a":
                    transpose_v(False, t_use(mix, j, ("v", 1)))
                for t in range(NS + 2):
                    if t < NS:
                        scores(mix, j, t)
                    before = {0: 0, 1: 1, 6: 1, 7: 1} if mix == "a" else {0: 1, 6: 1, 7: 1, NS: 3}
                    gemm(before.get(t, 2))
                    if 1 <= t <= NS:
                        transpose_p(mix, j, t - 1)
                    if t >= 2:
                        values(mix, j, t - 2)
                    if t == 6:
                        gemm(2)
                        cached_scores(mix, j)
                assert not k_steps

            pe.wait_ge(const_in, 64)
            pe.wait_ge(att_v_b, 16)
            transpose_v(True, 0, v_b)
            transpose_v(False, 1, v_b)
            with pe.Fori(0, PAIRS) as j:
                attention_pair("a", j)
            with pe.Fori(0, PAIRS) as j:
                attention_pair("b", j)

            with pe.Fori(0, N_PROJ // 2) as i:
                for s in range(2):
                    m = 2 * i + s
                    pe.wait_ge(split_done, U_PROJ + m + 1)
                    for z in range(2):
                        pe.wait_ge(z_taken, 2 * m + z + 1)
                        for k in range(8 * z, 8 * z + 8):
                            last = k_step(s, k, z, 8 * z, 8 * z + 7, 1)
                        last.then_inc((za_done, unit_done)[z], 1)

            with pe.Fori(0, N_OUT // 2) as i:
                for s in range(2):
                    unit(s, U_OUT + 2 * i + s, (r_done, 2 * i + s + 1), 2)

            def layer_norm(q):
                for (src, cols, out) in ln_parts[q]:
                    if q == 0:
                        last = pe.matmul(out(0), ones, lsum[:, cols], start=True, stop=True)
                    elif not cols.start:
                        last = pe.matmul(out(0), ones, psum, start=True, stop=True)
                    else:
                        pe.wait_ge(smp_ready, 1)
                        for k in range(KT_N):
                            last = pe.matmul(out(0), ones, src(k), start=(k == 0), stop=(k == KT_N - 1))
                last.then_inc(ln[q]["sum"], 1)
                for k in range(KT_N):
                    pe.wait_ge(ln[q]["squared"], k + 1)
                    for (src, cols, out) in ln_parts[q]:
                        last = pe.matmul(out(1), ones, sq_t[k % 2][:, cols], start=(k == 0), stop=(k == KT_N - 1))
                    last.then_inc(ln[q]["sq_used"], 1)

            pe.wait_ge(lsum_done, 1 + N_OUT)
            layer_norm(0)

            def key_scores(s, c):
                pe.wait_ge(q_evac, c + 3)
                pe.wait_ge(sc_taken, c + 1)
                four, one = sc_parts(s)
                for b in range(NB):
                    out = four[:, P * b:P * b + P] if b < 4 else one
                    last = pe.matmul(out, qe[s][:, P * b:P * b + P], subkt[:, KEYS * s:KEYS * s + KEYS],
                                     start=True, stop=True)
                last.then_inc(sc_full, 1)

            with pe.Fori(0, N_QUERY // 2) as i:
                unit(0, U_QUERY + 2 * i, (q_evac, 2 * i + 1), 3)
                pe.wait_ge(split_done, U_QUERY + 2 * i + 2)
                pe.wait_ge(q_evac, 2 * i + 2)
                for k in range(KT_N):
                    last = k_step(1, k, 1, 0, KT_N - 1, 3)
                    if k == 3:
                        key_scores(0, 2 * i)
                last.then_inc(unit_done, 1)
                key_scores(1, 2 * i + 1)

            def act_step(s, k, bank):
                for n, (a, b) in enumerate(((w_hi, mv_hi), (w_hi, mv_lo), (w_lo, mv_hi))):
                    last = pe.matmul(banks[:, bank, :], a[s][:, P * k:P * k + P], b[:, k, 0:SEQ],
                                     start=(k == 0 and n == 0), stop=(k == KT_N - 1 and n == 2))
                if k == KT_N - 1:
                    last.then_inc(unit_done, 1)

            pe.wait_ge(sc_taken, 2 + N_QUERY)
            pe.wait_ge(q_evac, 2 + N_QUERY)
            def tail_units(lo, hi):
                for n in range(lo, hi):
                    pe.wait_ge(split_done, U_PEER + n + 1)
                    if n >= 2:
                        pe.wait_ge(gelu_done, n - 1)
                    for k in range(KT_N):
                        act_step(n % 2, k, n % 2)

            tail_units(0, TAIL_PICKS)

            pe.wait_ge(picks_done, 1)
            for q, src in enumerate((pick_g, pick_e[0], pick_e[1])):
                for b in range(SEQ // P):
                    last = pe.transpose(banks[:, 4 + q, P * b:P * b + P], src[:, b, :], ident)
                last.then_inc(picks_full, 1)
            pe.wait_ge(picks_taken, 3)
            for k in range(KT_N):
                for n, part in enumerate((mv_hi, mv_lo)):
                    last = pe.matmul(nat[:, P * k:P * k + P], part[:, k, SEQ:T].bitcast(f32), ident,
                                     start=(n == 0), stop=(n == 1))
            last.then_inc(nat_ready, 1)
            tail_units(TAIL_PICKS, TAIL)

            pe.sem_inc(g_full, 2)
            with pe.Fori(0, GBLK // 2) as i:
                for q in range(2 * GT // 4):
                    for k in (2 * q, 2 * q + 1):
                        s, n = k // KT_N, TAIL + 2 * i + k // KT_N
                        if k % KT_N == 0:
                            pe.wait_ge(split_done, U_PEER + n + 1)
                            pe.wait_ge(gelu_done, n - 1)
                        act_step(s, k % KT_N, s)
                    pe.wait_ge(oh_ready, 16 * i + q + 1)
                    pe.wait_ge(g_evac, 16 * i + q + 1)
                    for t in range(4):
                        n = 4 * (q % 2) + t
                        last = pe.matmul(banks[:, 2 + q % 2, P * t:P * t + P], oh2[:, n, :].bitcast(f32), oh1[:, n, :],
                                         start=True, stop=True)
                    last.then_inc(g_full, 1)
            pe.wait_ge(g_evac, 2 + SEQ // 4)
            pe.wait_ge(gelu_done, N_EARLY)

            def out_units(g, q, first, early):
                def free(dt):
                    if dt < 4 and not early:
                        pe.wait_ge(gelu_done, 4 * g + dt + 1)
                    else:
                        pe.wait_ge(out_evac, 16 * q + dt + 1)

                def part(v, d, e):
                    for n, (a, b) in enumerate(((w_hi, ww_hi), (w_hi, ww_lo), (w_lo, ww_hi))):
                        at = P * (EG * d + e)
                        last = pe.matmul(banks[:, d, :], a[v % 2][:, at:at + P], b[:, e, :],
                                         start=(e == 0 and n == 0), stop=(e == EG - 1 and n == 2))
                    if e == EG - 1:
                        last.then_inc(unit_done if d == 3 else part_done, 1)

                pe.wait_ge(split_done, first + 1)
                for e in range(EG):
                    pe.wait_ge(w_ready, 4 * q + e + 3)
                    for d in range(4):
                        if e == 0:
                            free(d)
                        part(0, d, e)
                for v in range(1, EG):
                    pe.wait_ge(split_done, first + v + 1)
                    for d in range(4):
                        free(4 * v + d)
                        for e in range(EG):
                            part(v, d, e)

            def late_group(g, q, first):
                for e in range(EG):
                    pe.wait_ge(split_done, first + e + 1)
                    pe.wait_ge(out_evac, 16 * q + e + 1)
                    for k in range(KT_N):
                        act_step(e % 2, k, e)
                out_units(g, q, first + EG, False)

            with pe.Fori(0, EARLY) as i:
                late_group(EARLY + i, 2 * i, U_PEER + N_EARLY + 12 * i)
                out_units(i, 2 * i + 1, U_PEER + N_EARLY + 12 * i + 2 * EG, True)
            with pe.Fori(2 * EARLY, GROUPS) as g:
                late_group(g, g, U_PEER + 8 * g)

            pe.wait_ge(psum_done, KT_N)
            pe.wait_ge(nat_out, 1)
            pe.wait_ge(out_evac, 4 + KT_N * GROUPS)
            for k in range(KT_N):
                last = pe.transpose(nat[:, P * k:P * k + P], rows_t[0][:, P * k:P * k + P], ident)
            last.then_inc(nat_t, 1)

            layer_norm(1)

        @block.scalar
        def _(act):
            act.sem_inc(w_prod, 1)
            for first in (*qkv_stored, *gate_stored, *g_stored):
                act.sem_inc(first, 16)

            def load_moving(src, phase, after, after_last=()):
                for w in after:
                    act.wait_ge(*w)

                def load(q):
                    act.dma_start(Rt[:, 2 * q:2 * q + 2, :], src[2 * q:2 * q + 2].rearrange("k p t -> p k t")) \
                        .then_inc(mv_in[q], 16)

                for q in range(4):
                    load(q)
                for k in range(KT_N):
                    if k % 2 == 0:
                        act.wait_ge(mv_in[k // 2], 16 * phase + 16)
                        if k < 8:
                            if k == 6:
                                for w in after_last:
                                    act.wait_ge(*w)
                            load(k // 2 + 4)
                    act.activation(mv_hi[:, k, :], Rt[:, k, :], ACT.Copy).then_inc(mvh_done, 1)

            act.sem_inc(qkv_evac, 2)
            load_moving(x_t, 0, ())

            act.dma_start(cst[:, :], consts).then_inc(const_in, 16)
            act.dma_start(subkt[:, :], subk).then_inc(const_in, 16)
            act.dma_start(sinkt[:, :], sinks).then_inc(const_in, 16)
            act.dma_start(lnt[:, :], lnp).then_inc(const_in, 16)
            rt = rext.tensor
            n_r = rext.shape[1]
            act.dma_start(bp_a[:, 64:P, :], bass.AP(rt, 63, [[n_r, 16], [-1, 64], [1, 512]])).then_inc(tab_done, 16)
            act.dma_start(bp_a[:, 0:64, 0:448], bass.AP(rt, 127, [[n_r, 16], [-1, 64], [1, 448]])).then_inc(tab_done, 16)
            act.dma_start(bp_a[:, 0:64, 448:512], negs).then_inc(tab_done, 16)
            for b in range(DEC_B):
                act.dma_start(bs_a[:, DEC_T * b:DEC_T * b + DEC_T, :], bass.AP(rt, 383, [[n_r, 16], [-1, 16], [1, 144]])) \
                    .then_inc(tab_done, 16)

            def evacuate_qkv(i):
                for s in range(2):
                    act.wait_ge(unit_done, 2 * i + s + 1)
                    act.wait_ge(qkv_stored[s], 16 + 16 * i)
                    act.activation(two(ev[s]), acc(s), ACT.Copy).then_inc(qkv_evac, 1)
                    act.wait_ge(qkv_evac, 2 * i + s + 3)
                    act.dma_start(pt_out[ds(2 * i + s, 1)].rearrange("a p t -> p (a t)"), ev[s]) \
                        .then_inc(qkv_stored[s], 16)

            trips = (ROW_KB + 2) // 2
            with act.Fori(0, trips) as i:
                evacuate_qkv(i)
            act.wait_ge(qkv_stored[1], 16 + 16 * trips)
            act.wait_ge(mv_ready, KT_N)
            act.dma_start(v_b, pt_out[ROW_KB + 1]).then_inc(att_v_b, 16)
            with act.Fori(trips, N_QKV // 2) as i:
                evacuate_qkv(i)

            def gate_evacuate(n, s, trip):
                act.wait_ge(unit_done, U_GATE + n + 1)
                act.wait_ge(gate_stored[s], 16 + 16 * trip)
                act.activation(two(ev[s]), acc(s), ACT.Copy).then_inc(gate_evac, 1)
                act.wait_ge(gate_evac, n + 3)
                act.dma_start(g_s[ds(n, 1)].rearrange("a p t -> p (a t)"), ev[s]).then_inc(gate_stored[s], 16)

            def take(mix, j, what):
                kind, t = what
                if kind == "v":
                    src, dst = (t_bank[:, 0:512], vn[:, 0:512]) if t == 0 else (t_bank[:, 0:P], vn[:, 512:T])
                elif kind == "c":
                    src = t_bank[:, 0:2 * P].rearrange("p (b h t) -> p h b t", b=DEC_B, h=2)
                    dst = st_both.rearrange("p (h b t) -> p h b t", b=DEC_B, h=2)
                else:
                    w = width(mix, STEPS[t][1])
                    src, dst = t_bank[:, 0:w], pt_sb[t % 2][:, 0:w]
                    if t >= 2:
                        act.wait_ge(o_full, STEP_BASE[mix] + NS * j + t - 1)
                act.wait_ge(t_full, t_use(mix, j, what, 1))
                act.activation(dst, src, ACT.Copy).then_inc(t_taken, 1)

            def attention_pair(mix, j, pair):
                def load(dst, src, into):
                    act.dma_start(dst, src).then_inc(into, 16)

                def row(src, r):
                    return src[ds(r, 1)].rearrange("a p t -> p (a t)")

                if mix == "a":
                    load(v_t, row(pt_out, 8 + j), att_q)
                    load(q_t, row(pt_out, ROW_QA + j), att_q)
                    load(k_t, row(pt_out, j), att_q)
                    load(bp_t, bp_a[ds(2 * j, 2)].rearrange("h p c -> p h c"), att_b)
                    load(bs_t, bs_a[ds(2 * j, 2)].rearrange("h p c -> p h c"), att_b)
                    load(ck_t, row(cka, j), att_c)
                    load(cv_t, row(cva, j), att_c)
                else:
                    load(q_t, row(pt_out, ROW_QB + j), att_q)
                    load(bp_t[:, :, 256:512], bp_b[ds(2 * j, 2)].rearrange("h p c -> p h c"), att_b)
                    load(bs_t, bs_b[ds(2 * j, 2)].rearrange("h p c -> p h c"), att_b)
                if mix == "a":
                    take(mix, j, ("v", 0))
                    take(mix, j, ("v", 1))
                for t in range(NS + 1):
                    if t < NS:
                        w, step = width(mix, STEPS[t][1]), STEP_BASE[mix] + NS * j + t
                        act.wait_ge(nmax_ready, step + 1)
                        exp = act.activation(s_sb[t % 2][:, 0:w], s_sb[t % 2][:, 0:w], ACT.Exp, bias=nmax[t % 2],
                                             accum_out=rsum[t % 2])
                        if mix == "b":
                            col = 2 * j + STEPS[t][0]
                            exp = act.activation(esink[t % 2], sinkt[:, ds(col, 1)], ACT.Exp, bias=nmax[t % 2])
                        exp.then_inc(e_ready, 1)
                    if t >= 1:
                        take(mix, j, ("t", t - 1))
                    if t == 6:
                        take(mix, j, ("c", 0))
                    if t == 6:
                        gate_evacuate(2 * pair, 0, pair)
                act.wait_ge(o_taken, 1 + STEP_BASE[mix] + NS * j + NS)
                act.dma_start(y_s[ds(pair, 1)].rearrange("a p t -> p (a t)"), y_t).then_inc(y_stored, 16)
                gate_evacuate(2 * pair + 1, 1, pair)

            act.sem_inc(gate_evac, 2)
            for s in range(2):
                act.wait_ge(qkv_stored[s], 16 + 16 * (N_QKV // 2))
            act.wait_ge(tab_done, 16 * (3 + DEC_B))
            for n in range(2):
                act.wait_ge(t_full, 1 + n)
                src, dst = (t_bank[:, 0:512], vn_b[:, 0:512]) if n == 0 else (t_bank[:, 0:P], vn_b[:, 512:T])
                act.activation(dst, src, ACT.Copy).then_inc(t_taken, 1)
            with act.Fori(0, PAIRS) as j:
                attention_pair("a", j, j)
            for dst, src, into in ((k_t, pt_out[ROW_KB], att_q),
                                   (ck_t, ckb, att_c), (cv_t, cvb, att_c)):
                act.dma_start(dst, src).then_inc(into, 16)
            with act.Fori(0, PAIRS) as j:
                attention_pair("b", j, PAIRS + j)

            load_moving(y_s, 1, ((y_stored, 16 + 16 * (2 * PAIRS - 1)), (unit_done, U_PROJ)),
                        ((y_stored, 16 + 16 * 2 * PAIRS),))
            for s in range(2):
                act.wait_ge(gate_stored[s], 16 + 16 * 2 * PAIRS)
            with act.Fori(0, N_PROJ // 2) as i:
                for s in range(2):
                    m = 2 * i + s
                    act.wait_ge(msum_done, m + 1)
                    act.dma_start(gate_t[s].rearrange("p (a t) -> p a t", a=2),
                                  g_s[ds(2 * m, 2)].rearrange("a p t -> p a t")).then_inc(gate_in[s], 16)
                    act.wait_ge(gate_in[s], 16 * i + 16)
                    act.activation(gate_t[s], gate_t[s], ACT.Sigmoid).then_inc(sig_done, 1)

            act.wait_ge(msum_done, N_PROJ + 2)
            act.wait_ge(unit_done, U_OUT)
            for k in range(KT_N):
                act.activation(mv_hi[:, k, :], Rt[:, k, :], ACT.Copy).then_inc(mvh_done, 1)
            with act.Fori(0, N_OUT // 2) as i:
                for s in range(2):
                    act.wait_ge(r_done, 2 * i + s + 1)
                    act.dma_start(x_res[s], x_t[ds(2 * i + s, 1)].rearrange("a p t -> p (a t)")).then_inc(x_in[s], 16)

            def layer_norm(q, finish):
                for k in range(KT_N):
                    act.wait_ge(ln[q]["centered"], k + 1)
                    if k >= 2:
                        act.wait_ge(ln[q]["sq_used"], k - 1)
                    for (src, cols, out) in ln_parts[q]:
                        last = act.activation(sq_t[k % 2][:, cols], src(k), ACT.Square)
                    last.then_inc(ln[q]["squared"], 1)
                act.wait_ge(ln[q]["var"], 1)
                act.activation(rstd_t, rstd_t, ACT.Sqrt).then_inc(ln[q]["std"], 1)
                if q == 0:
                    act.sem_inc(q_evac, 2)
                for k in range(KT_N):
                    act.wait_ge(ln[q]["scaled"], k + 1)
                    finish(k, lnt[:, KT_N * (2 * q + 1) + k:KT_N * (2 * q + 1) + k + 1])

            act.wait_ge(const_in, 64)
            layer_norm(0, lambda k, shift: act.activation(mv_hi[:, k, :], Rt[:, k, :], ACT.Identity, bias=shift)
                       .then_inc(mvh_done, 1))

            act.wait_ge(mv_ready, 4 * KT_N)
            act.sem_inc(sc_taken, 2)
            with act.Fori(0, N_QUERY // 2) as i:
                for s in range(2):
                    c = 2 * i + s
                    act.wait_ge(unit_done, U_QUERY + c + 1)
                    act.activation(two(qe[s]), acc(s), ACT.Copy).then_inc(q_evac, 1)
                    act.wait_ge(sc_full, c + 1)
                    act.wait_ge(topk_done, c + 1)
                    four, one = sc_parts(s)
                    act.activation(sc_sb[s][:, 0:512], four, ACT.Copy)
                    act.activation(sc_sb[s][:, 512:T], one, ACT.Copy).then_inc(sc_taken, 1)

            def early_activation(n, s, trip):
                act.wait_ge(unit_done, U_PEER + n + 1)
                act.wait_ge(act_stored[s], 16 * trip)
                act.activation(act_t[s], banks[:, s, :], ACT.Gelu).then_inc(gelu_done, 1)
                act.wait_ge(gelu_done, n + 1)
                act.dma_start(a_s[ds(n, 1)].rearrange("a p t -> p (a t)"), act_t[s]).then_inc(act_stored[s], 16)

            for n in range(TAIL_PICKS - 2):
                early_activation(n, n % 2, n // 2)
            act.wait_ge(gexp_in, 1)
            flat = pick_g.rearrange("p b k -> p (b k)")
            act.activation(flat, flat, ACT.Exp).then_inc(gexp_done, 1)
            for n in range(TAIL_PICKS - 2, TAIL_PICKS):
                early_activation(n, n % 2, n // 2)
            for q in range(3):
                act.wait_ge(picks_full, q + 1)
                act.activation(pick_t[q], banks[:, 4 + q, :], ACT.Copy).then_inc(picks_taken, 1)
            for n in range(TAIL_PICKS, TAIL):
                early_activation(n, n % 2, n // 2)

            act.sem_inc(g_evac, 2)
            with act.Fori(0, GBLK // 2) as i:
                for q in range(2 * GT // 4):
                    w, qq = q // 8, q % 8
                    act.wait_ge(g_full, 16 * i + q + 3)
                    if qq == 0:
                        act.wait_ge(g_stored[w], 16 + 16 * i)
                    act.activation(g_buf[w][:, :, 4 * qq:4 * qq + 4],
                                   banks[:, 2 + q % 2, :].rearrange("p (t e) -> p e t", t=4), ACT.Copy).then_inc(g_evac, 1)
                    if qq == 7:
                        act.wait_ge(g_evac, 16 * i + q + 3)
                        act.dma_start(G_s[ds(2 * i + w, 1)].rearrange("a p e t -> p (a e t)"),
                                      g_buf[w].rearrange("p e t -> p (e t)")).then_inc(g_stored[w], 16)
                    if q in (8, 15):
                        early_activation(TAIL + 2 * i + q // 15, q // 15, TAIL // 2 + i)

            for w in range(2):
                act.wait_ge(g_stored[w], 16 + 16 * (GBLK // 2))
                act.wait_ge(act_stored[w], 16 * (N_EARLY // 2))

            def load_gates(g, q):
                act.wait_ge(w_prod, 1 + 4 * q)
                act.dma_start(G4.rearrange("p b e t -> p b (e t)"),
                              G_s[:, :, ds(EG * g, EG), :].rearrange("b p e t -> p b (e t)")).then_inc(g4_in, 16)

            def high_part(q, e):
                act.wait_ge(w_prod, 1 + 4 * q + e + 1)
                act.activation(ww_hi[:, e, :], act_t[e % 2], ACT.Copy).then_inc(wwh_done, 1)

            def early_group(g, q, used):
                load_gates(g, q)

                def load_act(e):
                    act.wait_ge(w_ready, 4 * q + e + 1)
                    act.dma_start(act_t[e % 2], a_s[ds(EG * g + e, 1)].rearrange("a p t -> p (a t)")) \
                        .then_inc(act_in[e % 2], 16)

                load_act(0)
                load_act(1)
                act.wait_ge(unit_done, used)
                for e in range(EG):
                    high_part(q, e)
                    if e < 2:
                        load_act(e + 2)

            def late_group(g, q, first):
                load_gates(g, q)
                for e in range(EG):
                    act.wait_ge(unit_done, first + e + 1)
                    act.wait_ge(w_ready, 4 * q + e + 1)
                    act.activation(act_t[e % 2], banks[:, e, :], ACT.Gelu).then_inc(gelu_done, 1)
                    high_part(q, e)

            with act.Fori(0, EARLY) as i:
                late_group(EARLY + i, 2 * i, U_PEER + N_EARLY + 12 * i)
                early_group(i, 2 * i + 1, U_PEER + N_EARLY + 12 * i + 2 * EG)
            with act.Fori(2 * EARLY, GROUPS // 2) as g:
                late_group(g, g, U_PEER + 8 * g)
            act.wait_ge(act_n_ready, 1)
            act.activation(act_n, act_n, ACT.Gelu).then_inc(act_n_gelu, 1)
            with act.Fori(GROUPS // 2, GROUPS) as g:
                late_group(g, g, U_PEER + 8 * g)

            act.wait_ge(nat_t, 1)
            for n in range(4):
                last = act.activation(rows_t[1][:, SEQ * n:SEQ * n + SEQ], banks[:, 4 + n, :], ACT.Copy)
            last.then_inc(smp_ready, 1)

            def store_y(k, shift):
                for (src, cols, out) in ln_parts[1]:
                    last = act.activation(src(k), src(k), ACT.Identity, bias=shift)
                last.then_inc(ln[1]["out"], 1)
                act.wait_ge(ln[1]["out"], k + 1)
                for (src, cols, out) in ln_parts[1]:
                    act.dma_start(y_out[k, :, cols], src(k)).then_inc(y_out_done, 16)

            layer_norm(1, store_y)
            act.wait_ge(y_out_done, 16 * 2 * KT_N)

        @block.vector
        def _(dve):
            own = Own(dve, dve_own, dve_apart)
            dve.sem_inc(lsum_done, 1)
            dve.sem_inc(y_stored, 16)

            def split_low(phase, free=None):
                for k in range(KT_N):
                    dve.wait_ge(mvh_done, KT_N * phase + k + 1)
                    if k == 0 and free is not None:
                        dve.sem_inc(free, 2)
                    dve.tensor_tensor(mv_lo[:, k, :], Rt[:, k, :], mv_hi[:, k, :].bitcast(f32), ALU.subtract) \
                        .then_inc(mv_ready, 1)

            dve.wait_ge(mv_in[0], 16)
            split_low(0)

            def soft_in(mix, j, t):
                hh, i = STEPS[t]
                w, step = width(mix, i), STEP_BASE[mix] + NS * j + t
                buf, bank = s_sb[t % 2], s_bank[t % 2]
                dve.wait_ge(s_full, step + 1)
                if t >= 2:
                    dve.wait_ge(t_full, t_use(mix, j, ("t", t - 2), 1))
                if i == "sample":
                    dve.scalar_tensor_tensor(buf[:, 0:P], bank[:, 0:P], SCALE, bs_t[:, hh, 0:P], ALU.mult, ALU.add)
                    dve.scalar_tensor_tensor(buf[:, P:2 * P], bank[:, P:2 * P], SCALE, bmask, ALU.mult, ALU.add) \
                        .then_inc(s_taken, 1)
                    dve.wait_ge(s_taken, 1 + step + 1)
                    new = buf[:, P:2 * P].rearrange("p (b t) -> p b t", b=DEC_B)
                    own.done(dve.tensor_tensor(new, new, bs_t[:, hh, P:P + DEC_T].unsqueeze(1)
                                               .to_broadcast([P, DEC_B, DEC_T]), ALU.add))
                    own.wait()
                else:
                    dve.scalar_tensor_tensor(buf[:, 0:w], bank[:, 0:w], SCALE, bp_t[:, hh, 512 - P * (w // P):512]
                                             if mix == "b" else bp_t[:, hh, 384 - P * i:512], ALU.mult, ALU.add) \
                        .then_inc(s_taken, 1)
                    dve.wait_ge(s_taken, 1 + step + 1)
                if mix == "a":
                    dve.tensor_reduce(nmax[t % 2], buf[:, 0:w], AX.X, ALU.max, negate=True).then_inc(nmax_ready, 1)
                else:
                    own.done(dve.tensor_reduce(mx[t % 2], buf[:, 0:w], AX.X, ALU.max))
                    own.wait()
                    dve.tensor_scalar(nmax[t % 2], mx[t % 2], sinkt[:, ds(2 * j + hh, 1)], -1.0, ALU.max, ALU.mult) \
                        .then_inc(nmax_ready, 1)

            def soft_out(mix, j, t):
                w = width(mix, STEPS[t][1])
                dve.wait_ge(e_ready, STEP_BASE[mix] + NS * j + t + 1)
                total = rsum[t % 2]
                if mix == "b":
                    own.done(dve.tensor_tensor(den[t % 2], rsum[t % 2], esink[t % 2], ALU.add))
                    own.wait()
                    total = den[t % 2]
                own.done(dve.reciprocal(rden[t % 2], total))
                own.wait()
                dve.tensor_scalar(s_sb[t % 2][:, 0:w], s_sb[t % 2][:, 0:w], rden[t % 2], None, ALU.mult) \
                    .then_inc(p_ready, 1)

            def out_take(mix, j, t, pair):
                hh, i = STEPS[t]
                rows, at = slice(HD * hh, HD * hh + HD), SEQ if i == "sample" else P * i
                if t == 0:
                    dve.wait_ge(y_stored, 16 + 16 * pair)
                dve.wait_ge(o_full, STEP_BASE[mix] + NS * j + t + 1)
                dve.tensor_copy(y_t[rows, at:at + P], o_bank[rows, 0:P]).then_inc(o_taken, 1)

            dve.wait_ge(const_in, 64)
            own.done(dve.memset(W2[:, 2 * T:2 * T + 2 * P], 0.0))
            own.wait()
            for mix in "ab":
                with dve.Fori(0, PAIRS) as j:
                    own.enter(j, 2 + NS * (1 if mix == "a" else 3))
                    dve.wait_ge(att_q, Q_BASE[mix] + Q_PER[mix] * j + Q_PER[mix])
                    for hh in range(2):
                        rows = slice(HD * hh, HD * hh + HD)
                        last = dve.tensor_copy(q_both[rows, :, hh, :],
                                               q_t[rows, SEQ:T].rearrange("p (b t) -> p b t", b=DEC_B))
                    last.then_inc(q_both_ready, 1)
                    dve.wait_ge(att_b, BIAS_BASE[mix] + 32 * j + 32)
                    for t in range(NS + 2):
                        if 1 <= t <= NS:
                            soft_out(mix, j, t - 1)
                        if t < NS:
                            soft_in(mix, j, t)
                        if t >= 2:
                            out_take(mix, j, t - 2, j + (PAIRS if mix == "b" else 0))
                    own.leave(PAIRS)

            split_low(1, z_taken)
            dve.sem_inc(msum_done, 2)
            with dve.Fori(0, N_PROJ // 2) as i:
                for s in range(2):
                    m = 2 * i + s
                    ga, gb = gate_t[s][:, 0:T], gate_t[s][:, T:2 * T]
                    dve.wait_ge(sig_done, m + 1)
                    dve.wait_ge(za_done, m + 1)
                    dve.tensor_tensor(two(ga), acc(0), two(ga), ALU.mult).then_inc(z_taken, 1)
                    dve.wait_ge(unit_done, U_PROJ + m + 1)
                    dve.tensor_tensor(two(gb), acc(1), two(gb), ALU.mult).then_inc(z_taken, 1)
                    dve.wait_ge(z_taken, 2 * m + 4)
                    dve.tensor_tensor(R[:, ds(T * m, T)], ga, gb, ALU.add).then_inc(msum_done, 1)

            split_low(2, r_done)
            own.done(dve.memset(lsum, 0.0))
            with dve.Fori(0, N_OUT // 2) as i:
                for s in range(2):
                    m = 2 * i + s
                    dve.wait_ge(lsum_done, 1 + m)
                    dve.wait_ge(x_in[s], 16 * i + 16)
                    dve.wait_ge(unit_done, U_OUT + m + 1)
                    dve.scalar_tensor_tensor(two(R[:, ds(T * m, T)]), two(x_res[s]), ALPHA, acc(s), ALU.mult, ALU.add) \
                        .then_inc(r_done, 1)
                    dve.wait_ge(r_done, m + 3)
                    dve.tensor_tensor(lsum, lsum, R[:, ds(T * m, T)], ALU.add).then_inc(lsum_done, 1)

            def layer_norm(q):
                wide = [(cols, [out(z) for z in range(2)]) for (src, cols, out) in ln_parts[q]]
                dve.wait_ge(ln[q]["sum"], 1)
                for cols, out in wide:
                    last = dve.tensor_scalar(mean_t[:, cols], out[0], 1.0 / D, None, ALU.mult)
                own.done(last)
                own.wait()
                parts = ln_parts[q] if q else [(lambda k: Rt[:, k, :], slice(0, T), None)]
                for k in range(KT_N):
                    for (src, cols, _) in parts:
                        last = dve.tensor_tensor(src(k), src(k), mean_t[:, cols], ALU.subtract)
                    last.then_inc(ln[q]["centered"], 1)
                dve.wait_ge(ln[q]["sq_used"], KT_N)
                for cols, out in wide:
                    last = dve.tensor_scalar(rstd_t[:, cols], out[1], 1.0 / D, EPS, ALU.mult, ALU.add)
                last.then_inc(ln[q]["var"], 1)
                dve.wait_ge(ln[q]["std"], 1)
                own.done(dve.reciprocal(rstd_t, rstd_t))
                own.wait()
                dve.wait_ge(ln[q]["centered"], KT_N)
                for k in range(KT_N):
                    for (src, cols, _) in parts:
                        last = dve.scalar_tensor_tensor(src(k), src(k), lnt[:, 2 * KT_N * q + k:2 * KT_N * q + k + 1],
                                                        rstd_t[:, cols], ALU.mult, ALU.mult)
                    last.then_inc(ln[q]["scaled"], 1)
                    if q == 0 and k:
                        split_shifted(k - 1)

            def split_shifted(k):
                dve.wait_ge(mvh_done, KT_N * 3 + k + 1)
                dve.scalar_tensor_tensor(mv_lo[:, k, :], Rt[:, k, :], lnt[:, KT_N + k:KT_N + k + 1],
                                         mv_hi[:, k, :].bitcast(f32), ALU.add, ALU.subtract).then_inc(mv_ready, 1)

            layer_norm(0)
            split_shifted(KT_N - 1)

            def top16(n, src, alt, out_v, out_i):
                for b in range(NB):
                    last = dve.max(out_v(b)[:, 0:8], src(b))
                own.done(last)
                own.wait_apart()
                for b in range(NB):
                    dve.max_index(out_i(b)[:, 0:8], out_v(b)[:, 0:8], src(b))
                    last = dve.match_replace(alt(b), out_v(b)[:, 0:8], src(b), -3e38)
                own.done(last)
                own.wait_apart()
                for b in range(NB):
                    last = dve.max(out_v(b)[:, 8:16], alt(b))
                own.done(last)
                own.wait_apart()
                for b in range(NB):
                    last = dve.max_index(out_i(b)[:, 8:16], out_v(b)[:, 8:16], alt(b))
                return last

            dve.sem_inc(topk_done, 2)
            cand4 = cand.rearrange("p (b i j) -> p b i j", b=NB, i=TOPK)
            eq3 = eq.rearrange("p (n k) -> p n k", k=TOPK)
            eq4 = eq.rearrange("p (b n k) -> p b n k", b=NB, n=TOPK)
            full = [P, NB, TOPK, TOPK]
            with dve.Fori(0, N_QUERY // 2) as i:
                own.enter(i, 6 + 1 + 3 + 1 + 2 + 6)
                for s in range(2):
                    dve.wait_ge(sc_taken, 2 * i + s + 3)
                    dve.sem_inc(dve_apart, 1)
                    top16(KEYS, lambda b: sc_sb[s][:, P * b:P * b + P], lambda b: sc2[:, P * b:P * b + P],
                          lambda b: val[:, b, s, :], lambda b: idx_u[:, b, s, :]).then_inc(topk_done, 1)
                dve.wait_ge(topk_done, 2 * i + 4)
                dve.tensor_copy(idx_f, idx_u)
                own.done(dve.tensor_tensor(cand4, val[:, :, 0, :].unsqueeze(3).to_broadcast(full),
                                           val[:, :, 1, :].unsqueeze(2).to_broadcast(full), ALU.add))
                own.wait_apart()
                own.done(top16(TOPK * TOPK, lambda b: cand[:, 256 * b:256 * b + 256], lambda b: cand2[:, 256 * b:256 * b + 256],
                               lambda b: top_v[:, TOPK * b:TOPK * b + TOPK], lambda b: ci_u[:, TOPK * b:TOPK * b + TOPK]))
                own.wait()
                dve.tensor_copy(pick_g[:, :, ds(TOPK * i, TOPK)], top_v.rearrange("p (b k) -> p b k", b=NB))
                dve.tensor_scalar(cp_u[0], ci_u, 4, None, ALU.logical_shift_right)
                own.done(dve.tensor_scalar(cp_u[1], ci_u, TOPK - 1, None, ALU.bitwise_and))
                own.wait()
                dve.tensor_copy(c_f[0], cp_u[0])
                own.done(dve.tensor_copy(c_f[1], cp_u[1]))
                own.wait()
                for z in range(2):
                    own.done(dve.tensor_tensor(eq3, c_f[z].unsqueeze(2).to_broadcast([P, NB * TOPK, TOPK]),
                                               iota[:, 0:TOPK].unsqueeze(1).to_broadcast([P, NB * TOPK, TOPK]),
                                               ALU.is_equal))
                    own.wait()
                    own.done(dve.tensor_tensor(eq4, eq4, idx_f[:, :, z, :].unsqueeze(2).to_broadcast(full), ALU.mult))
                    own.wait()
                    own.done(dve.tensor_reduce(pick_e[z][:, :, ds(TOPK * i, TOPK)], eq4, AX.X, ALU.add))
                    own.wait()
                own.leave(N_QUERY // 2)

            g3 = pick_g.rearrange("p b (h k) -> p (b h) k", k=TOPK)
            own.wait()
            gm = cand[:, 0:NB * PH]
            own.done(dve.tensor_copy(gm.unsqueeze(2), g3[:, :, 0:1]))
            own.wait()
            wide = [P, NB * PH, TOPK]
            dve.tensor_tensor(g3, g3, gm.unsqueeze(2).to_broadcast(wide), ALU.subtract).then_inc(gexp_in, 1)
            dve.wait_ge(gexp_done, 1)
            own.done(dve.tensor_reduce(psum_g, g3, AX.X, ALU.add))
            own.wait()
            own.done(dve.reciprocal(psum_g, psum_g))
            own.wait()
            dve.tensor_tensor(g3, g3, psum_g.unsqueeze(2).to_broadcast(wide), ALU.mult).then_inc(picks_done, 1)
            dve.wait_ge(picks_done, 1)
            dve.tensor_copy(gate_n, pick_g[:, NB - 1, :])
            dve.scalar_tensor_tensor(idx_n, pick_e[0][:, NB - 1, :], float(KEYS), pick_e[1][:, NB - 1, :],
                                     ALU.mult, ALU.add).then_inc(idx_ready, 1)

            dve.wait_ge(picks_taken, 3)
            with dve.Fori(0, GBLK // 2) as i:
                for q in range(2 * GT // 4):
                    dve.wait_ge(g_full, 16 * i + q + 1)
                    for t in range(4):
                        n = 4 * (q % 2) + t
                        tok = ds(2 * GT * i + 4 * q + t, 1)
                        dve.tensor_scalar(oh2[:, n, :], iota, pick_t[2][:, tok], None, ALU.is_equal)
                        last = dve.tensor_scalar(oh1[:, n, :], iota, pick_t[1][:, tok], pick_t[0][:, tok],
                                                 ALU.is_equal, ALU.mult)
                    last.then_inc(oh_ready, 1)

            dve.wait_ge(g_full, 2 + SEQ // 4)
            dve.wait_ge(nat_ready, 1)
            dve.sem_inc(out_evac, 4)
            dve.sem_inc(w_ready, 2)
            dve.sem_inc(rows_used, 2)
            for w in range(2):
                dve.wait_ge(g_stored[w], 16 + 16 * (GBLK // 2))
            own.done(dve.tensor_scalar(r_acc, mv_hi[:, :, 0:SEQ].bitcast(f32), ALPHA, None, ALU.mult))
            own.wait()
            own.done(dve.scalar_tensor_tensor(r_acc, mv_lo[:, :, 0:SEQ].bitcast(f32), ALPHA, r_acc, ALU.mult, ALU.add))
            own.wait()

            def gather_step(table, g, c):
                rows = rows_t[c % 2]
                dve.wait_ge(rows_in[c % 2], 16 * (STEPS_G // 2 * g + c // 2 + 1))
                if table == "u":
                    ins = dve.tensor_tensor_reduce(rows, rows, nat, 1.0, 0.0, ALU.mult, ALU.add, dots[:, c:c + 1])
                else:
                    dve.wait_ge(rows_used, STEPS_G * g + c + 2)
                    w = act_n[:, ds(STEPS_G * (g - GROUPS // 2) + c, 1)]
                    ins = dve.scalar_tensor_tensor(nat, rows, w, nat, ALU.mult, ALU.add)
                ins.then_inc(rows_used, 1)
                if table == "u" and c == STEPS_G - 1:
                    dve.wait_ge(rows_used, STEPS_G * g + c + 3)
                    own.done(dve.tensor_copy(act_n[:, ds(STEPS_G * g, STEPS_G)], dots[:, :]))
                    own.wait()

            def product(e):
                a3 = act_t[e % 2].rearrange("p (b t) -> p b t", b=GBLK)
                dve.tensor_tensor(a3, a3, G4[:, :, e, :], ALU.mult).then_inc(w_prod, 1)

            def low_part(q, e):
                dve.wait_ge(wwh_done, 4 * q + e + 1)
                dve.tensor_tensor(ww_lo[:, e, :], act_t[e % 2], ww_hi[:, e, :].bitcast(f32), ALU.subtract) \
                    .then_inc(w_ready, 1)

            def add_out(q, v, first, sums=False):
                for d in range(4):
                    dt = 4 * v + d
                    if d < 3:
                        dve.wait_ge(part_done, 12 * q + 3 * v + d + 1)
                    else:
                        dve.wait_ge(unit_done, first + v + 1)
                    dve.tensor_tensor(r_acc[:, dt, :], r_acc[:, dt, :], banks[:, dt % 4, :], ALU.add) \
                        .then_inc(out_evac, 1)
                    if sums:
                        dve.wait_ge(out_evac, 16 * q + dt + 5)
                        if dt == 0:
                            dve.wait_ge(w_ready, 4 * q + 6)
                            dve.tensor_copy(psum, r_acc[:, 0, :]).then_inc(psum_done, 1)
                        else:
                            dve.wait_ge(psum_done, dt)
                            dve.tensor_tensor(psum, psum, r_acc[:, dt, :], ALU.add).then_inc(psum_done, 1)

            def late_group(g, q, first, steps, before_last=None, sums=False):
                dve.wait_ge(g4_in, 16 * q + 16)
                for e in range(EG):
                    steps(e)
                    dve.wait_ge(gelu_done, 4 * g + e + 1)
                    product(e)
                    low_part(q, e)
                for v in range(EG):
                    steps(EG + v)
                    if v == EG - 1 and before_last:
                        before_last()
                    add_out(q, v, first + EG, sums)

            with dve.Fori(0, EARLY) as i:
                own.enter(i, 2)

                def mixed(n):
                    for c in MIXED_STEPS[n]:
                        gather_step("u", 2 * i + c // STEPS_G, c % STEPS_G)

                def early_product(e):
                    if e == 0:
                        dve.wait_ge(g4_in, 32 * i + 32)
                    dve.wait_ge(act_in[e % 2], 16 * (2 * i + e // 2 + 1))
                    product(e)

                def first_products():
                    for e in range(2):
                        early_product(e)

                late_group(EARLY + i, 2 * i, U_PEER + N_EARLY + 12 * i, mixed, first_products)
                for e in range(EG):
                    if e >= 2:
                        early_product(e)
                    low_part(2 * i + 1, e)
                for v in range(EG):
                    mixed(2 * EG + v)
                    add_out(2 * i + 1, v, U_PEER + N_EARLY + 12 * i + 2 * EG)
                own.leave(EARLY)
            with dve.Fori(2 * EARLY, GROUPS // 2) as g:
                own.enter(g - 2 * EARLY, 1)
                late_group(g, g, U_PEER + 8 * g, lambda n: gather_step("u", g, n))
                own.leave(GROUPS // 2 - 2 * EARLY)
            own.wait()
            own.done(dve.tensor_scalar(nat, nat, ALPHA, None, ALU.mult))
            own.wait()
            dve.sem_inc(act_n_ready, 1)
            dve.wait_ge(act_n_gelu, 1)
            own.done(dve.tensor_tensor(act_n, act_n, gate_n, ALU.mult))
            own.wait()
            with dve.Fori(GROUPS // 2, GROUPS - 1) as g:
                late_group(g, g, U_PEER + 8 * g, lambda n: gather_step("v", g, n))
            g = GROUPS - 1
            late_group(g, g, U_PEER + 8 * g, lambda n: gather_step("v", g, n), sums=True)

            dve.wait_ge(rows_used, 2 + STEPS_G * GROUPS)
            dve.tensor_copy(rows_t[0], nat).then_inc(nat_out, 1)
            layer_norm(1)


def kernel(**inputs):
    import concourse.bacc as _bacc
    from concourse import mybir as _mybir
    from concourse.bass_utils import run_bass_kernel_spmd as _run

    a = {k: np.asarray(v) for k, v in inputs.items()}
    f = np.float32
    x = np.concatenate([a["x_prompt"].reshape(SEQ, D), a["x_sample"].reshape(-1, D)], 0)
    x_t = np.ascontiguousarray(x.T).reshape(KT_N, P, T)

    order = np.array([h for j in range(PAIRS) for h in (j, PAIRS + j)])

    def units(w):
        rows, cols = w.shape
        return w.reshape(rows // P, P, cols // P, P).transpose(2, 1, 0, 3).reshape(cols // P, P, rows)

    w_in = a["w_in"]
    cut = np.cumsum([0, 1024, 1024, 1024, 1024, 128, 128, 2048, 2048])
    qa, ka, va, qb, kb, vb, ga, gb = (w_in[:, cut[i]:cut[i + 1]] for i in range(8))
    qb = qb.reshape(D, 16, HD)[:, order].reshape(D, 1024)
    wpb = a["w_proj_b"].reshape(16, HD, D)[order].reshape(1024, D)
    ws = np.empty((UNITS, P, D), f)
    ws[U_QKV:U_GATE] = np.concatenate([units(w) for w in (ka, va, kb, vb, qa, qb)], 0)
    ws[U_GATE:U_PROJ:2] = units(ga)
    ws[U_GATE + 1:U_PROJ:2] = units(gb)
    ws[U_PROJ:U_OUT] = units(np.concatenate([a["w_proj_a"], wpb], 0))
    ws[U_OUT:U_QUERY] = units(a["w_out"])
    ws[U_QUERY:U_PEER] = units(a["peer_w_query"])
    u = a["peer_u"].reshape(GROUPS, EG, KEYS, KT_N, P).transpose(0, 1, 4, 3, 2).reshape(GROUPS, EG, P, D)
    v = a["peer_v"].reshape(GROUPS, EG, KEYS, 4, 4, P).transpose(0, 3, 2, 4, 1, 5).reshape(GROUPS, EG, P, D)
    ws[U_PEER:U_PEER + N_EARLY] = u[:EARLY].reshape(-1, P, D)
    mixed = ws[U_PEER + N_EARLY:U_PEER + 4 * N_EARLY].reshape(EARLY, 3, EG, P, D)
    mixed[:, 0], mixed[:, 1], mixed[:, 2] = u[EARLY:2 * EARLY], v[EARLY:2 * EARLY], v[:EARLY]
    late = ws[U_PEER + 4 * N_EARLY:].reshape(GROUPS - 2 * EARLY, 2, EG, P, D)
    late[:, 0], late[:, 1] = u[2 * EARLY:], v[2 * EARLY:]

    cka = a["cache_a_k"].reshape(DEC_B, PAST, PAIRS, 2 * HD).transpose(2, 3, 0, 1).reshape(PAIRS, P, DEC_B * PAST)
    cva = a["cache_a_v"].reshape(DEC_B, PAST, PAIRS, 2 * HD).transpose(2, 1, 0, 3).reshape(PAIRS, P, DEC_B * P)
    ckb = a["cache_b_k"].reshape(DEC_B, PAST, 2 * HD).transpose(2, 0, 1).reshape(P, DEC_B * PAST)
    cvb = a["cache_b_v"].reshape(DEC_B, PAST, 2 * HD).transpose(1, 0, 2).reshape(P, DEC_B * P)

    rext = np.pad(a["rel_bias_table"], ((0, 0), (0, 383)), mode="edge")[:, ::-1]
    negs = np.full((16, 64, 64), NEG, f)
    slope = np.exp2(-8.0 * np.arange(1, 17) / 16).astype(f)[order]
    q, c = np.arange(P)[:, None], np.arange(256)[None]
    seen = (q + P) // 64 - c // 64
    bp_b = np.where((seen >= 0) & (seen <= 2), -slope[:, None, None] * np.abs(q + P - c).astype(f), f(NEG)).astype(f)
    bs_b = (-slope[:, None, None] * np.abs(q % DEC_T + PAST - np.arange(144)[None]).astype(f)).astype(f)
    bmask = np.where(q // DEC_T == np.arange(P)[None] // DEC_T, f(0), f(NEG))
    consts = np.concatenate([np.eye(P), np.ones((P, P)), np.tile(np.arange(P), (P, 1)), bmask], 1).astype(f)
    sinks = np.tile(a["b_sinks"][order][None], (P, 1))
    lnp = np.concatenate([a[n].reshape(KT_N, P).T for n in ("ln1_g", "ln1_b", "ln2_g", "ln2_b")], 1)
    subk = np.concatenate([a["peer_sub_keys_1"].T, a["peer_sub_keys_2"].T], 1)

    nc = _bacc.Bacc("TRN2", target_bir_lowering=False, num_devices=1)
    arrays, args = {}, []
    for name, arr in (("x_t", x_t), ("wstream", ws), ("u_rows", a["peer_u"]), ("v_rows", a["peer_v"]), ("cka", cka), ("cva", cva), ("ckb", ckb), ("cvb", cvb),
                      ("rext", rext), ("negs", negs), ("bp_b", bp_b), ("bs_b", bs_b), ("sinks", sinks), ("lnp", lnp),
                      ("subk", subk), ("consts", consts)):
        arrays["in_" + name] = np.ascontiguousarray(arr)
        args.append(nc.dram_tensor("in_" + name, arr.shape, _mybir.dt.from_np(arr.dtype), kind="ExternalInput").ap())
    args.append(nc.dram_tensor("out_p", (N_QKV, P, T), _mybir.dt.float32, kind="ExternalOutput").ap())
    args.append(nc.dram_tensor("out_y", (KT_N, P, T), _mybir.dt.float32, kind="ExternalOutput").ap())
    build(nc, *args)
    r = _run(nc, [arrays], core_ids=[0]).results[0]
    p = np.asarray(r["out_p"])
    y = np.asarray(r["out_y"]).reshape(D, T).T

    def heads(lo, n):
        return np.ascontiguousarray(p[lo:lo + n].reshape(n * P, T).T).reshape(T, n * 2, HD)

    k_a, v_a, k_b, v_b = heads(0, 8), heads(8, 8), heads(16, 1), heads(17, 1)
    prompt = lambda t, n: np.ascontiguousarray(t[SEQ - n:SEQ])[None]
    sample = lambda t: np.ascontiguousarray(t[SEQ:]).reshape((DEC_B, DEC_T) + t.shape[1:])
    return (np.ascontiguousarray(y[:SEQ])[None], np.ascontiguousarray(y[SEQ:]).reshape(DEC_B, DEC_T, D),
            prompt(k_a, SEQ), prompt(v_a, SEQ), prompt(k_b, 128), prompt(v_b, 128),
            sample(k_a), sample(v_a), sample(k_b), sample(v_b))
```
